# Optimizing a Trainium2 kernel written in Bass

```python
import math
import jax, jax.numpy as jnp
from jax import lax
import numpy as np

D_MODEL = 1024
BATCH = 1
SEQ = 1024
DEPTH = 2

CHUNK = 64
Q_BLOCK = 128
HEAD_DIM = 64
ROPE_THETA = 10000.0
EPS = 1e-6
N_HEADS_TOTAL = D_MODEL // HEAD_DIM

SB_HEADS = N_HEADS_TOTAL // 4
SB_WIDTH = SB_HEADS * HEAD_DIM
SW_HEADS = N_HEADS_TOTAL // 2
SW_KV_HEADS = SW_HEADS // 4
SW_WINDOW = 128
SW_WINDOW_CHUNKS = SW_WINDOW // CHUNK
SW_WIDTH = SW_HEADS * HEAD_DIM
ML_HEADS = N_HEADS_TOTAL // 4
ML_NOPE = HEAD_DIM
ML_ROPE = HEAD_DIM // 2
ML_V = HEAD_DIM
ML_Q_RANK = D_MODEL // 4
ML_KV_RANK = D_MODEL // 8
ML_WIDTH = ML_HEADS * ML_V

MIX_WIDTH = SB_WIDTH + SW_WIDTH + ML_WIDTH
D_FF = 4 * D_MODEL

IN_SB = 3 * SB_WIDTH
IN_SW = SW_WIDTH + 2 * SW_KV_HEADS * HEAD_DIM
IN_ML = ML_Q_RANK + ML_KV_RANK + ML_ROPE
IN_WIDTH = IN_SB + IN_SW + IN_ML

kernel_name = "hybrid_stickbreak_swa_mla_block"

def rms_norm(x, g):
    xf = x.astype(jnp.float32)
    y = xf * lax.rsqrt(jnp.mean(xf * xf, axis=-1, keepdims=True) + EPS)
    return (y * g.astype(jnp.float32)).astype(x.dtype)

def rope_tables(seq, dim):
    inv = 1.0 / (ROPE_THETA ** (jnp.arange(0, dim, 2, dtype=jnp.float32) / dim))
    ang = jnp.arange(seq, dtype=jnp.float32)[:, None] * inv[None, :]
    return jnp.cos(ang), jnp.sin(ang)

def apply_rope(x, cos, sin):
    half = x.shape[-1] // 2
    c = cos[None, :, None, :].astype(x.dtype)
    s = sin[None, :, None, :].astype(x.dtype)
    x1, x2 = x[..., :half], x[..., half:]
    return jnp.concatenate([x1 * c - x2 * s, x1 * s + x2 * c], axis=-1)

def stick_breaking_attention(q, k, v):
    B, S, H, D = q.shape
    nb = S // Q_BLOCK
    scale = D ** -0.5
    key_pos = jnp.arange(S)
    q_blocks = q.reshape(B, nb, Q_BLOCK, H, D).transpose(1, 0, 2, 3, 4)

    def block(args):
        q_blk, b = args
        z = jnp.einsum('bqhd,bkhd->bhqk', q_blk, k).astype(jnp.float32) * scale
        q_pos = b * Q_BLOCK + jnp.arange(Q_BLOCK)
        mask = key_pos[None, :] < q_pos[:, None]
        log_rem = jnp.where(mask, jax.nn.log_sigmoid(-z), 0.0)
        between = lax.cumsum(log_rem, axis=3, reverse=True) - log_rem
        w = jnp.where(mask, jnp.exp(jax.nn.log_sigmoid(z) + between), 0.0)
        return jnp.einsum('bhqk,bkhd->bqhd', w.astype(v.dtype), v)

    out = lax.map(block, (q_blocks, jnp.arange(nb)))
    return out.transpose(1, 0, 2, 3, 4).reshape(B, S, H * D)

def sliding_window_sink_attention(q, k, v, sinks):
    B, S, H, D = q.shape
    KV = k.shape[2]
    G = H // KV
    NC = S // CHUNK
    W = SW_WINDOW_CHUNKS
    scale = D ** -0.5
    qc = q.reshape(B, NC, CHUNK, KV, G, D)
    pad = ((0, 0), (W - 1, 0), (0, 0), (0, 0), (0, 0))
    kp = jnp.pad(k.reshape(B, NC, CHUNK, KV, D), pad)
    vp = jnp.pad(v.reshape(B, NC, CHUNK, KV, D), pad)
    k_win = jnp.concatenate([kp[:, i:i + NC] for i in range(W)], axis=2)
    v_win = jnp.concatenate([vp[:, i:i + NC] for i in range(W)], axis=2)
    scores = jnp.einsum('bcqkgd,bcskd->bckgqs', qc, k_win).astype(jnp.float32) * scale
    key_chunk = jnp.arange(NC)[:, None] - (W - 1) + jnp.arange(W * CHUNK)[None, :] // CHUNK
    valid = (key_chunk >= 0)[None, :, None, None, None, :]
    scores = jnp.where(valid, scores, -jnp.inf)
    sink = jnp.broadcast_to(sinks.astype(jnp.float32).reshape(1, 1, KV, G, 1, 1),
                            scores.shape[:-1] + (1,))
    probs = jax.nn.softmax(jnp.concatenate([scores, sink], axis=-1), axis=-1)[..., :-1]
    out = jnp.einsum('bckgqs,bcskd->bcqkgd', probs.astype(v.dtype), v_win)
    return out.reshape(B, S, H * D)

def latent_attention(q_nope, q_rope, k_nope, k_rope, v):
    B, S, H, _ = q_nope.shape
    nb = S // Q_BLOCK
    scale = (ML_NOPE + ML_ROPE) ** -0.5
    key_chunk = jnp.arange(S) // CHUNK
    qn_b = q_nope.reshape(B, nb, Q_BLOCK, H, ML_NOPE).transpose(1, 0, 2, 3, 4)
    qr_b = q_rope.reshape(B, nb, Q_BLOCK, H, ML_ROPE).transpose(1, 0, 2, 3, 4)

    def block(args):
        qn, qr, b = args
        s = (jnp.einsum('bqhd,bkhd->bhqk', qn, k_nope)
             + jnp.einsum('bqhr,bkr->bhqk', qr, k_rope)).astype(jnp.float32) * scale
        q_chunk = (b * Q_BLOCK + jnp.arange(Q_BLOCK)) // CHUNK
        mask = key_chunk[None, :] <= q_chunk[:, None]
        p = jax.nn.softmax(jnp.where(mask, s, -jnp.inf), axis=-1)
        return jnp.einsum('bhqk,bkhd->bqhd', p.astype(v.dtype), v)

    out = lax.map(block, (qn_b, qr_b, jnp.arange(nb)))
    return out.transpose(1, 0, 2, 3, 4).reshape(B, S, H * ML_V)

def hybrid_layer(x, cos_sw, sin_sw, cos_ml, sin_ml, attn_norm, w_in, mla_q_norm, mla_kv_norm,
                 w_mla_uq, w_mla_ukv, sink_logits, group_norm, w_out, mlp_norm, w_mlp_in, w_mlp_out):
    B, S, _ = x.shape
    h = rms_norm(x, attn_norm)
    p = h @ w_in
    p_sb = p[..., :IN_SB]
    p_sw = p[..., IN_SB:IN_SB + IN_SW]
    p_ml = p[..., IN_SB + IN_SW:]

    q_a, k_a, v_a = [t.reshape(B, S, SB_HEADS, HEAD_DIM) for t in jnp.split(p_sb, 3, axis=-1)]
    o_a = stick_breaking_attention(q_a, k_a, v_a)

    kv_w = SW_KV_HEADS * HEAD_DIM
    q_b = apply_rope(p_sw[..., :SW_WIDTH].reshape(B, S, SW_HEADS, HEAD_DIM), cos_sw, sin_sw)
    k_b = apply_rope(p_sw[..., SW_WIDTH:SW_WIDTH + kv_w].reshape(B, S, SW_KV_HEADS, HEAD_DIM), cos_sw, sin_sw)
    v_b = p_sw[..., SW_WIDTH + kv_w:].reshape(B, S, SW_KV_HEADS, HEAD_DIM)
    o_b = sliding_window_sink_attention(q_b, k_b, v_b, sink_logits)

    c_q = rms_norm(p_ml[..., :ML_Q_RANK], mla_q_norm)
    c_kv = rms_norm(p_ml[..., ML_Q_RANK:ML_Q_RANK + ML_KV_RANK], mla_kv_norm)
    k_r = p_ml[..., ML_Q_RANK + ML_KV_RANK:]
    q_c = (c_q @ w_mla_uq).reshape(B, S, ML_HEADS, ML_NOPE + ML_ROPE)
    kv_c = (c_kv @ w_mla_ukv).reshape(B, S, ML_HEADS, ML_NOPE + ML_V)
    q_nope = q_c[..., :ML_NOPE]
    q_rope = apply_rope(q_c[..., ML_NOPE:], cos_ml, sin_ml)
    k_rope = apply_rope(k_r[:, :, None, :], cos_ml, sin_ml)[:, :, 0, :]
    o_c = latent_attention(q_nope, q_rope, kv_c[..., :ML_NOPE], k_rope, kv_c[..., ML_NOPE:])

    o_a = rms_norm(o_a, group_norm[:SB_WIDTH])
    o_b = rms_norm(o_b, group_norm[SB_WIDTH:SB_WIDTH + SW_WIDTH])
    o_c = rms_norm(o_c, group_norm[SB_WIDTH + SW_WIDTH:])
    x = x + jnp.concatenate([o_a, o_b, o_c], axis=-1) @ w_out

    hm = rms_norm(x, mlp_norm)
    x = x + jnp.square(jax.nn.relu(hm @ w_mlp_in)) @ w_mlp_out
    return x

def setup_inputs(seed: int = 0) -> dict:
    key = jax.random.key(seed)
    ks = jax.random.split(key, 16)

    def nrm(k, shape, scale):
        return jax.random.normal(k, shape, jnp.float32) * scale

    def gain(k, shape):
        return 1.0 + 0.02 * jax.random.normal(k, shape, jnp.float32)

    return {
        "x": nrm(ks[0], (BATCH, SEQ, D_MODEL), 1.0),
        "attn_norm": gain(ks[1], (DEPTH, D_MODEL)),
        "w_in": nrm(ks[2], (DEPTH, D_MODEL, IN_WIDTH), D_MODEL ** -0.5),
        "mla_q_norm": gain(ks[3], (DEPTH, ML_Q_RANK)),
        "mla_kv_norm": gain(ks[4], (DEPTH, ML_KV_RANK)),
        "w_mla_uq": nrm(ks[5], (DEPTH, ML_Q_RANK, ML_HEADS * (ML_NOPE + ML_ROPE)), ML_Q_RANK ** -0.5),
        "w_mla_ukv": nrm(ks[6], (DEPTH, ML_KV_RANK, ML_HEADS * (ML_NOPE + ML_V)), ML_KV_RANK ** -0.5),
        "sink_logits": nrm(ks[7], (DEPTH, SW_HEADS), 0.5),
        "group_norm": gain(ks[8], (DEPTH, MIX_WIDTH)),
        "w_out": nrm(ks[9], (DEPTH, MIX_WIDTH, D_MODEL), MIX_WIDTH ** -0.5),
        "mlp_norm": gain(ks[10], (DEPTH, D_MODEL)),
        "w_mlp_in": nrm(ks[11], (DEPTH, D_MODEL, D_FF), D_MODEL ** -0.5),
        "w_mlp_out": nrm(ks[12], (DEPTH, D_FF, D_MODEL), D_FF ** -0.5),
        "final_norm": gain(ks[13], (D_MODEL,)),
    }

def reference(x, attn_norm, w_in, mla_q_norm, mla_kv_norm, w_mla_uq, w_mla_ukv, sink_logits,
              group_norm, w_out, mlp_norm, w_mlp_in, w_mlp_out, final_norm):
    S = x.shape[1]
    cos_sw, sin_sw = rope_tables(S, HEAD_DIM)
    cos_ml, sin_ml = rope_tables(S, ML_ROPE)
    for l in range(DEPTH):
        x = hybrid_layer(x, cos_sw, sin_sw, cos_ml, sin_ml, attn_norm[l], w_in[l], mla_q_norm[l],
                         mla_kv_norm[l], w_mla_uq[l], w_mla_ukv[l], sink_logits[l], group_norm[l],
                         w_out[l], mlp_norm[l], w_mlp_in[l], w_mlp_out[l])
    return rms_norm(x, final_norm)


_drawn_inputs = setup_inputs


def setup_inputs(seed=0):
    import zlib

    import numpy as np

    out = dict(_drawn_inputs(seed))
    spreads = {}
    factors = {'mla_q_norm': 8.0,
     'mla_kv_norm': 4.655,
     'sink_logits': 8.0,
     'group_norm': 3.171,
     'mlp_norm': 3.036,
     'final_norm': 2.711}
    for name, (base, spread) in spreads.items():
        noise = np.random.default_rng([zlib.crc32(name.encode()), seed]).standard_normal(out[name].shape)
        drawn = base * np.exp(spread * noise) if base else spread * noise
        out[name] = __import__('jax').numpy.asarray(drawn.astype(out[name].dtype))
    for name, factor in factors.items():
        out[name] = (out[name] * factor).astype(out[name].dtype)
    return out
```

```python
from contextlib import ExitStack

import concourse.bass as bass
from concourse import mybir

F32 = mybir.dt.float32
F32R = mybir.dt.float32r
BF16 = mybir.dt.bfloat16
ALU = mybir.AluOpType
ACT = mybir.ActivationFunctionType
AX_X = mybir.AxisListType.X

P = 128
D = 1024
S = 1024
DEPTH = 2
NT = S // P
NK = D // P
HALF = 512
HD = 64
EPS = 1e-6
BIG = -1e30

A_HEADS, B_HEADS, C_HEADS = 4, 8, 4
ROPE_C = 32
QK_C = HD + ROPE_C
Q_RANK, KV_RANK = 256, 128
QA, KA, VA = 0, 256, 512
QB, KB, VB = 768, 1280, 1408
CQ, CKV, KR = 1536, 1792, 1920
IN_W = 1952
OC = CQ

BLOCKS = [HALF, HALF, HALF, IN_W - 3 * HALF]
D_FF = 4096
NF = D_FF // P
NC = NF // 2

U_IN, U_OUT, U_MLP = 16, 8, 2 * NF
U_ALL = U_IN + U_OUT + U_MLP
U_M = U_IN + U_OUT

SCALE_A = HD ** -0.5
SCALE_C = QK_C ** -0.5


class Count:

    def __init__(self, const=0, terms=()):
        self.const, self.terms = const, tuple(terms)

    def __add__(self, other):
        if isinstance(other, Count):
            return Count(self.const + other.const, self.terms + other.terms)
        return Count(self.const + other, self.terms)

    __radd__ = __add__

    def __sub__(self, other):
        return self + (-other)

    def __mul__(self, by):
        return Count(self.const * by, [(var, k * by) for var, k in self.terms])

    __rmul__ = __mul__


class Waiter:

    def __init__(self, eng, name, apart=None):
        self.eng, self.name, self.regs, self.apart = eng, name, None, apart

    def wait_ge(self, semaphore, count, apart=None):
        if not isinstance(count, Count):
            return self.eng.wait_ge(semaphore, count)
        if self.regs is None:
            self.regs = [self.eng.alloc_register(f"{self.name}_{what}") for what in ("total", "part", "count")]
        total, part, reached = self.regs
        for n, (var, k) in enumerate(count.terms):
            self.eng.reg_mul(part if n else total, var, k)
            if n:
                self.eng.reg_add(total, total, part)
        assert count.const > 0, "a wait on a register's value is never on zero"
        self.eng.reg_add(reached, total, count.const)
        self.eng.wait_ge(semaphore, reached)
        apart = apart or self.apart
        if apart:
            self.eng.sem_inc(apart, 1)


def hybrid_trunk(nc, x_in, attn_norm, w_in, mla_q_norm, mla_kv_norm, w_mla_uq, w_mla_ukv, sink_logits,
                 group_norm, w_out, mlp_norm, w_mlp_in, w_mlp_out, final_norm,
                 ident_in, causal_in, chunk_in, rope_b_in, rope_c_in, out, depth=DEPTH):
    ctx = ExitStack()
    with ctx:
        start = (nc.sbuf_base + 127) // 128 * 128
        arena = {"at": start}

        def region(size):
            at = arena["at"]
            arena["at"] += size
            return at

        X, HT, PR, WA, RAW, CO = (region(k * 1024) for k in (32, 64, 64, 32, 8, 0))

        def place(name, shape, dt, offset):
            return nc.alloc_sbuf_tensor_at(name, shape, dt, offset=offset)

        KB_ = 1024
        x = place("x", [P, NT, D], F32, X)
        hT_hi = place("hT_hi", [P, NK, S], F32R, HT)
        hT_lo = place("hT_lo", [P, NK, S], F32R, HT + 32 * KB_)
        p = place("p", [P, NT, IN_W], F32, PR)
        ws_hi = [place("wsa_hi", [P, 4, 1024], F32R, WA), place("wsb_hi", [P, 4, 1024], F32R, PR)]
        ws_lo = [place("wsa_lo", [P, 4, 1024], F32R, WA + 16 * KB_),
                 place("wsb_lo", [P, 4, 1024], F32R, PR + 16 * KB_)]
        aT_hi = place("aT_hi", [P, 4, S], F32R, PR + 32 * KB_)
        aT_lo = place("aT_lo", [P, 4, S], F32R, PR + 48 * KB_)
        hn = place("hn", [P, 2, D], F32, PR + 48 * KB_)
        raw = place("raw", [P, 2, 1024], F32, RAW)

        e_buf = place("e_buf", [P, 2, S], F32, HT)
        c_buf = place("c_buf", [P, 2, S], F32, HT + 8 * KB_)
        w_buf = place("w_buf", [P, 2, S], F32, HT + 16 * KB_)
        wT = place("wT", [P, 2, S], F32, HT + 24 * KB_)
        cqT = place("cqT", [P, 2, S], F32, HT)
        ckvT = place("ckvT", [P, S], F32, HT + 8 * KB_)
        w_ukv = place("w_ukv", [P, HALF], F32, HT + 12 * KB_)
        qk_asm = place("qk_asm", [P, 2, 2, C_HEADS, QK_C], F32, HT + 16 * KB_)
        rope_t = place("rope_t", [P, 2, 2, C_HEADS, ROPE_C], F32, HT + 22 * KB_)
        w_uq = place("w_uq", [P, 2, C_HEADS * QK_C], F32, HT + 28 * KB_)
        junk_q = place("junk_q", [P, NT, Q_RANK], F32, HT + 16 * KB_)
        junk_kv = place("junk_kv", [P, NT, KV_RANK], F32, HT + 24 * KB_)
        junk_g = place("junk_g", [P, NT, 1024], F32, HT)
        masks_in = place("masks_in", [P, 2, P], F32, HT)
        qT_A = place("qT_A", [P, 2, S], F32, HT + 32 * KB_)
        kT_A = place("kT_A", [P, 2, S], F32, HT + 40 * KB_)
        qT_B = place("qT_B", [P, 4, S], F32, HT + 32 * KB_)
        kT_C = place("kT_C", [P, C_HEADS, S], F32, HT + 32 * KB_)
        rope_b = place("rope_b", [P, NT, 2, HD], F32, HT + 48 * KB_)
        rb1 = place("rb1", [P, 10, HD], F32, HT + 56 * KB_)
        rb2 = place("rb2", [P, 10, HD], F32, HT + 60 * KB_)
        KPAD = HD + S
        kT_B = place("kT_B", [P, KPAD], F32, HT + 48 * KB_)
        kT_Bs = place("kT_Bs", [P, KPAD], F32, HT + 48 * KB_ + 4 * KPAD)
        v_Bs = place("v_Bs", [P, NT, P], F32, HT + 48 * KB_ + 8 * KPAD)
        qT_C = place("qT_C", [P, C_HEADS, S], F32, HT + 48 * KB_)

        def const(name, shape, dt):
            size = 2 if dt == BF16 else 4
            for n in shape[1:]:
                size *= n
            at = region((size + 31) // 32 * 32)
            assert at + size <= nc.sbuf_usable_end, (name, at + size - nc.sbuf_usable_end)
            return place(name, shape, dt, at)

        gain = const("gain", [P, 1024], F32)
        relu_t = place("relu_t", [P, 2, HALF], F32, CO)
        ident = const("ident", [P, P], F32)
        identb = const("identb", [P, P], BF16)
        causal = const("causal", [P, P], BF16)
        chunk = const("chunk", [P, P], BF16)
        rope_c = const("rope_c", [P, NT, 2, ROPE_C], F32)
        sink = const("sink", [P, B_HEADS], F32)
        nsink = const("nsink", [P, B_HEADS], F32)
        ms = const("ms", [P, NT], F32)
        rs = const("rs", [P, NT], F32)
        gms = const("gms", [P, 3, NT], F32)
        grs = const("grs", [P, 3, NT], F32)
        power = const("power", [P, 3, NT], F32)
        top = const("top", [P, 2, B_HEADS], F32)
        ntop = const("ntop", [P, 2, B_HEADS], F32)
        psm = place("psm", [P, NT, B_HEADS], F32, PR + NT * IN_W * 4)
        rden = place("rden", [P, NT, B_HEADS], F32, PR + NT * IN_W * 4 + NT * B_HEADS * 4)

        bank = [ctx.enter_context(nc.psum_tensor(f"bank{i}", [P, 2, HALF], F32)) for i in range(4)]

        def B(i):
            return bank[i // 2][:, i % 2, :]

        def pair(i):
            return bank[i][:, :, :].rearrange("p a n -> p (a n)")

        def sem(name):
            return ctx.enter_context(nc.semaphore(name))

        consts_in, masks_ready = sem("consts_in"), sem("masks_ready")
        x_loaded = [sem(f"x_loaded{t}") for t in range(NT)]
        raw_loaded = [sem("raw_loaded0"), sem("raw_loaded1")]
        gain_loaded, sink_loaded, tab_loaded, up_loaded = (sem(n) for n in (
            "gain_loaded", "sink_loaded", "tab_loaded", "up_loaded"))
        hi_split, split_done, in_used = sem("hi_split"), sem("split_done"), sem("in_used")
        sq_done, rstd_done, hn_done, norm_tr, hT_hi_done, hT_lo_done = (sem(n) for n in (
            "sq_done", "rstd_done", "hn_done", "norm_tr", "hT_hi_done", "hT_lo_done"))
        proj_done, p_act, p_dve = sem("proj_done"), sem("p_act"), sem("p_dve")
        rope_step = sem("rope_step")
        ta_tr, ta_act, ta_dve = sem("ta_tr"), sem("ta_act"), sem("ta_dve")
        tb_tr, tb_act, tb_dve, tb_fill = sem("tb_tr"), sem("tb_act"), sem("tb_dve"), sem("tb_fill")
        tc_sq, tc_rs, tc_n = sem("tc_sq"), sem("tc_rs"), sem("tc_n")
        sp_passed, pool_passed, pe_passed = sem("sp_passed"), sem("pool_passed"), sem("pe_passed")
        power_set, eps_added = sem("power_set"), sem("eps_added")
        tc_tr, tc_act, tc_dve = sem("tc_tr"), sem("tc_act"), sem("tc_dve")
        up_done, up_act, up_dve, asm_tr, asm_act, asm_dve = (sem(n) for n in (
            "up_done", "up_act", "up_dve", "asm_tr", "asm_act", "asm_dve"))
        z_done, w_done, t_done, te_act, te_dve, pv_done, o_done = (
            {g: sem(f"{n}_{g}") for g in "ABC"} for n in (
                "z_done", "w_done", "t_done", "te_act", "te_dve", "pv_done", "o_done"))
        a_step, l_done, d_done, top_done = sem("a_step"), sem("l_done"), sem("d_done"), sem("top_done")
        topc_done, es_done = sem("topc_done"), sem("es_done")
        g_sq, g_rs, g_n, oT_tr, oT_hi, oT_lo = (sem(n) for n in ("g_sq", "g_rs", "g_n", "oT_tr", "oT_hi", "oT_lo"))
        wo_done, wadd_done = sem("wo_done"), sem("wadd_done")
        mu_done, relu_done, msq_done, mhi_done, mlo_done, md_done, madd_done = (sem(n) for n in (
            "mu_done", "relu_done", "msq_done", "mhi_done", "mlo_done", "md_done", "madd_done"))
        layer_ready = sem("layer_ready")
        dve_chain, stored = sem("dve_chain"), [sem("stored0"), sem("stored1")]

        units = {"A": [(h, b) for h in range(A_HEADS) for b in range(NT)],
                 "B": [(None, t) for t in range(NT)],
                 "C": [(h, b) for h in range(C_HEADS) for b in range(NT)]}
        NU = {g: len(u) for g, u in units.items()}

        def key_tiles(g, u):
            return B_HEADS if g == "B" else units[g][u][1] + 1

        def nth(g, u, odd):
            return (u + 1) // 2 if odd else u // 2 + 1

        def wait_moved(eng, g, L, u):
            half = NU[g] // 2
            if u % 2 == 0:
                eng.wait_ge(te_act[g], L * half + nth(g, u, False))
            else:
                eng.wait_ge(te_dve[g], L * half + nth(g, u, True))

        def b_cols(h):
            return (h % 2) * HALF + (h // 2) * P

        slot_of = [u % 4 for u in range(U_IN)] + list(range(U_OUT))
        mlp_order = [("up", 0, 0), ("up", 0, 1)]
        for c in range(NC):
            if c + 1 < NC:
                mlp_order += [("up", c + 1, 0), ("up", c + 1, 1)]
            mlp_order += [("down", c, 0), ("down", c, 1)]
        slot_of += [(c % 2) * 4 + (0 if kind == "up" else 2) + f for kind, c, f in mlp_order]

        def W(slot, lo=False):
            return (ws_lo if lo else ws_hi)[slot // 4][:, slot % 4, :]

        with nc.Block() as block:

            @block.sync
            def _(sp_engine):
                sp = Waiter(sp_engine, "sp", apart=sp_passed)
                for dst, src in ((ident[:, :], ident_in), (masks_in[:, 0, :], causal_in), (masks_in[:, 1, :], chunk_in),
                                 (rope_c[:, :, :, :], rope_c_in)):
                    sp_engine.dma_start(dst, src).then_inc(consts_in, 16)
                for t in range(NT):
                    sp_engine.dma_start(x[:, t, :], x_in[0, t * P:(t + 1) * P, :]).then_inc(x_loaded[t], 16)

                def land(u, L, src, width=1024, split=1):
                    if u >= 2:
                        sp.wait_ge(split_done, L * U_ALL + u - 1)
                    dst = raw[:, u % 2, 0:width]
                    if split > 1:
                        dst = dst.rearrange("p (k n) -> p k n", k=split)
                    sp_engine.dma_start(dst, src).then_inc(raw_loaded[u % 2], 16)

                def layer(L_reg, L):
                    w_in_l = w_in[bass.ds(L_reg, 1), :, :].rearrange("a (k p) n -> p (a k) n", p=P)
                    w_out_l = w_out[bass.ds(L_reg, 1), :, :].rearrange("a (k p) n -> p (a k) n", p=P)
                    w1_l = w_mlp_in[bass.ds(L_reg, 1), :, :].rearrange("a (k p) n -> p (a k) n", p=P)

                    def w2(f):
                        return w_mlp_out[bass.ds(L_reg, 1), bass.ds(f * P, P), :].rearrange("a p n -> p (a n)")

                    def w1(f):
                        return w1_l[:, :, bass.ds(f * P, P)]

                    def load_gain(src, at, width):
                        sp_engine.dma_start(gain[:, at:at + width], src[bass.ds(L_reg, 1), :].rearrange("a n -> (a n)")
                                     .partition_broadcast(P)).then_inc(gain_loaded, 16)

                    load_gain(attn_norm, 0, D)
                    for a in range(2):
                        sp_engine.dma_start(sink[:, 4 * a:4 * a + 4],
                                     sink_logits[bass.ds(L_reg, 1), bass.ds(a, 4, 2)].rearrange("a h -> (a h)")
                                     .partition_broadcast(P),
                                     allow_slow_non_contiguous=True).then_inc(sink_loaded, 16)
                    for u in range(U_IN):
                        j, i = u // 4, u % 4
                        width = BLOCKS[j]
                        land(u, L, w_in_l[:, 2 * i:2 * i + 2, j * HALF:j * HALF + width], 2 * width, 2)
                    sp.wait_ge(hn_done, (2 * L + 1) * NT)
                    load_gain(mla_q_norm, 0, Q_RANK)
                    load_gain(mla_kv_norm, Q_RANK, KV_RANK)
                    for u in (16, 17):
                        land(u, L, w_out_l[:, 2 * (u - 16):2 * (u - 16) + 2, 0:HALF], 1024, 2)
                    sp.wait_ge(proj_done, (L + 1) * 4 * NT)
                    sp_engine.dma_start(rope_b[:], rope_b_in).then_inc(tab_loaded, 16)
                    for u in (18, 19, 20, 21):
                        i, j = (u - 16) % 4, (u - 16) // 4
                        land(u, L, w_out_l[:, 2 * i:2 * i + 2, j * HALF:(j + 1) * HALF], 1024, 2)
                    sp.wait_ge(o_done["B"], (L + 1) * NU["B"])
                    sp_engine.dma_start(w_uq[:, :, :], w_mla_uq[bass.ds(L_reg, 1), :, :]
                                 .rearrange("a (k p) n -> p (a k) n", p=P)).then_inc(up_loaded, 16)
                    sp_engine.dma_start(w_ukv[:, :], w_mla_ukv[bass.ds(L_reg, 1), :, :]
                                 .rearrange("a p n -> p (a n)")).then_inc(up_loaded, 16)
                    sp.wait_ge(tc_n, (L + 1) * 2 * NT)
                    load_gain(group_norm, 0, D)
                    for u in (22, 23):
                        i, j = (u - 16) % 4, (u - 16) // 4
                        land(u, L, w_out_l[:, 2 * i:2 * i + 2, j * HALF:(j + 1) * HALF], 1024, 2)
                    sp.wait_ge(g_n, (L + 1) * 3 * NT)
                    load_gain(mlp_norm, 0, D)

                    v = U_M

                    def land_w1(v, f):
                        land(v, L, w1(f), 1024, NK)

                    for c, f in ((0, 0), (0, 1), (1, 0), (1, 1)):
                        land_w1(v, 2 * c + f)
                        v += 1
                    for f in range(2):
                        land(v, L, w2(f))
                        v += 1
                    with sp_engine.Fori(0, NC // 2 - 1) as i_reg:
                        i = Count(0, [(i_reg, 1)])
                        for k in range(2):
                            for n in range(4):
                                first = U_M + 6 + 4 * k + n
                                sp.wait_ge(split_done, L * U_ALL + 8 * i + (first - 1))
                                if n < 2:
                                    sp_engine.dma_start(raw[:, first % 2, :].rearrange("p (k n) -> p k n", k=NK),
                                                 w1(4 * i_reg + (4 + 2 * k + n))).then_inc(raw_loaded[first % 2], 16)
                                else:
                                    sp_engine.dma_start(raw[:, first % 2, :],
                                                 w2(4 * i_reg + (2 + 2 * k + n - 2))).then_inc(raw_loaded[first % 2], 16)
                    for f in range(2):
                        land(U_ALL - 2 + f, L, w2(NF - 2 + f))
                    sp.wait_ge(split_done, (L + 1) * U_ALL)
                    sp.wait_ge(msq_done, (L + 1) * 4 * NC)

                with sp_engine.Fori(0, depth) as L:
                    layer(L, Count(0, [(L, 1)]))
                sp_engine.dma_start(gain[:, 0:D], final_norm.partition_broadcast(P)).then_inc(gain_loaded, 16)
                for t in range(NT):
                    sp.wait_ge(hn_done, 2 * depth * NT + t + 1)
                    sp_engine.dma_start(out[0, t * P:(t + 1) * P, :], hn[:, t % 2, :]).then_inc(stored[t % 2], 16)
                for b in range(2):
                    sp.wait_ge(stored[b], 8 * NT)

            @block.gpsimd
            def _(pool_engine):
                pool = Waiter(pool_engine, "pool", apart=pool_passed)
                def unit(L, u, width=1024, used=None):
                    slot = slot_of[u]
                    if used is not None:
                        pool.wait_ge(*used)
                    pool.wait_ge(raw_loaded[u % 2], L * (8 * U_ALL) + 16 * (u // 2 + 1))
                    nc.gpsimd.tensor_copy(W(slot)[:, 0:width], raw[:, u % 2, 0:width]).then_inc(hi_split, 1)
                    pool.wait_ge(hi_split, L * U_ALL + u + 1)
                    nc.gpsimd.tensor_tensor(W(slot, True)[:, 0:width], raw[:, u % 2, 0:width],
                                            W(slot)[:, 0:width].bitcast(F32), ALU.subtract).then_inc(split_done, 1)

                added = [0]

                def root(L, mean, r, count_done):
                    nc.gpsimd.tensor_scalar(r, mean, EPS, 1.0, ALU.add, ALU.mult).then_inc(eps_added, 1)
                    added[0] += 1
                    pool.wait_ge(eps_added, L * ROOTS + added[0])
                    exponent = power[:, 0:r.shape[1], :] if len(r.shape) == 3 else power[:, 0, 0:1]
                    nc.gpsimd.tensor_tensor(r, r, exponent, ALU.pow).then_inc(count_done, 1)

                ROOTS = 2 * NT + 2

                def norm_roots(L, L2):
                    for t in range(NT):
                        pool.wait_ge(sq_done, L2 * NT + t + 1)
                        root(L, ms[:, t:t + 1], rs[:, t:t + 1], rstd_done)

                def projected(L, u):
                    j, i = u // 4, u % 4
                    return (in_used, L * 12 + 3 * j + i + 1) if i < 3 else (proj_done, L * 4 * NT + NT * (j + 1))

                def layer(L_reg, L):
                    added[0] = 0
                    for u in range(U_IN):
                        if u == 4:
                            norm_roots(L, 2 * L)
                        unit(L, u, 2 * BLOCKS[u // 4], projected(L, u - 4) if u >= 4 else None)
                    for u in range(16, 20):
                        unit(L, u, 1024, projected(L, u - 4))
                    pool.wait_ge(p_act, (L + 1) * 2 * NT)
                    pool.wait_ge(p_dve, (L + 1) * 2 * NT)
                    pool.wait_ge(tab_loaded, (L + 1) * 16)
                    n = 0
                    for t in range(NT):
                        for v, half, cos, sin, m1, m2 in (
                            (p[:, t, QB:VB].rearrange("p (h d) -> p h d", d=HD), HD // 2,
                             rope_b[:, t, 0:1, :], rope_b[:, t, 1:2, :], rb1[:, :, :], rb2[:, :, :]),
                            (p[:, t, KR:IN_W].rearrange("p (h d) -> p h d", d=ROPE_C), ROPE_C // 2,
                             rope_c[:, t, 0:1, :], rope_c[:, t, 1:2, :], rb1[:, 0:1, 0:ROPE_C],
                             rb2[:, 0:1, 0:ROPE_C])):
                            heads, width = v.shape[1], 2 * half
                            nc.gpsimd.tensor_tensor(m1, v, cos.to_broadcast([P, heads, width]),
                                                    ALU.mult).then_inc(rope_step, 1)
                            for a in range(2):
                                nc.gpsimd.tensor_tensor(
                                    m2[:, :, a * half:(a + 1) * half], v[:, :, (1 - a) * half:(2 - a) * half],
                                    sin[:, :, a * half:(a + 1) * half].to_broadcast([P, heads, half]),
                                    ALU.mult).then_inc(rope_step, 1)
                            n += 3
                            pool.wait_ge(rope_step, L * (2 * 4 * NT) + n)
                            nc.gpsimd.tensor_tensor(v, m1, m2, ALU.add).then_inc(rope_step, 1)
                            n += 1
                            pool.wait_ge(rope_step, L * (2 * 4 * NT) + n)
                    pool.wait_ge(tc_sq, (L + 1) * NT)
                    root(L, gms[:, 0:2, :], grs[:, 0:2, :], tc_rs)
                    pool.wait_ge(g_sq, (L + 1) * NT)
                    root(L, gms[:, :, :], grs[:, :, :], g_rs)
                    pool.wait_ge(oT_tr, (L + 1) * 2 * NT)
                    for u in range(20, 24):
                        unit(L, u)
                    for v in range(6):
                        if v == 2:
                            norm_roots(L, 2 * L + 1)
                        unit(L, U_M + v, 1024,
                             (wo_done, L * 2 * NT + NT * (1 if slot_of[U_M + v] < 4 else 2)))
                    G, M = L * 4 * NC, L * 16 * NC
                    with pool_engine.Fori(0, NC // 2 - 1) as i_reg:
                        i = Count(0, [(i_reg, 1)])
                        for m in range(8):
                            first = U_M + 6 + m
                            s, s2 = slot_of[first], first % 2
                            if m % 4 < 2:
                                pool.wait_ge(mu_done, G + 8 * i + (m - m % 4 + 2 * (m % 4 + 1)))
                            else:
                                pool.wait_ge(md_done, M + 32 * i + (16 * (m // 4) or 1))
                            pool.wait_ge(raw_loaded[s2], L * (8 * U_ALL) + 64 * i + 16 * (first // 2 + 1))
                            nc.gpsimd.tensor_copy(W(s), raw[:, s2, :]).then_inc(hi_split, 1)
                            pool.wait_ge(hi_split, L * U_ALL + 8 * i + (first + 1))
                            nc.gpsimd.tensor_tensor(W(s, True), raw[:, s2, :], W(s).bitcast(F32),
                                                    ALU.subtract).then_inc(split_done, 1)
                    for f in range(2):
                        unit(L, U_ALL - 2 + f, 1024, (md_done, M + 16 * (NC - 2)))
                    pool.wait_ge(md_done, M + 16 * (NC - 1))
                    assert added[0] == ROOTS

                nc.gpsimd.memset(power[:, :, :], -0.5).then_inc(power_set, 1)
                pool.wait_ge(power_set, 1)
                with pool_engine.Fori(0, depth) as L:
                    layer(L, Count(0, [(L, 1)]))
                added[0] = 0
                norm_roots(depth, 2 * depth)

            @block.scalar
            def _(act_engine):
                act = Waiter(act_engine, "act")
                nc.scalar.preload_act_table_set("natural_log_exp_and_others")
                def norm_row(L2, t, x_ready):
                    x_ready()
                    if t >= 2:
                        act.wait_ge(norm_tr, L2 * 2 * NT + 2 * (t - 1))
                    nc.scalar.activation(hn[:, t % 2, :], x[:, t, :], ACT.Square, scale=D ** -0.5,
                                         accum_out=ms[:, t:t + 1]).then_inc(sq_done, 1)

                def hT_high(L2, t):
                    for j in range(2):
                        q = 2 * t + j
                        act.wait_ge(norm_tr, L2 * 2 * NT + q + 1)
                        nc.scalar.activation(hT_hi[:, 4 * j:4 * j + 4, t * P:(t + 1) * P],
                                             B(4 + q % 4).rearrange("p (k n) -> p k n", k=4),
                                             ACT.Copy).then_inc(hT_hi_done, 1)

                def norm(L2, x_ready):
                    for t in range(NT):
                        norm_row(L2, t, lambda t=t: x_ready(t))
                        if t >= 1:
                            hT_high(L2, t - 1)
                    hT_high(L2, NT - 1)

                def move_T(g, L, u):
                    act.wait_ge(t_done[g], L * NU[g] + u + 1)
                    n = key_tiles(g, u) * P
                    nc.scalar.activation(wT[:, u % 2, 0:n], pair(2)[:, 0:n], ACT.Copy).then_inc(te_act[g], 1)

                def layer(L_reg, L):
                    def x_ready(t):
                        act.wait_ge(x_loaded[t], 16)
                        act.wait_ge(layer_ready, L + 1)
                    norm(2 * L, x_ready)

                    for j in range(4):
                        for t in range(0, NT, 2):
                            act.wait_ge(proj_done, L * 4 * NT + NT * j + t + 1)
                            nc.scalar.activation(p[:, t, j * HALF:j * HALF + BLOCKS[j]], B(t)[:, 0:BLOCKS[j]],
                                                 ACT.Copy).then_inc(p_act, 1)

                    for i in range(0, 8, 2):
                        act.wait_ge(ta_tr, L * 8 + i + 1)
                        dst = (qT_A if i < 4 else kT_A)[:, (i // 2) % 2, 0:HALF]
                        nc.scalar.activation(dst, B(i), ACT.Copy,
                                             scale=SCALE_A if i < 4 else 1.0).then_inc(ta_act, 1)

                    def softplus_part(u):
                        n = key_tiles("A", u) * P
                        e = e_buf[:, u % 2, 0:n]
                        act.wait_ge(z_done["A"], L * NU["A"] + u + 1)
                        nc.scalar.activation(e, pair(u % 2)[:, 0:n], ACT.Abs).then_inc(a_step, 1)
                        act.wait_ge(a_step, L * 2 * NU["A"] + 2 * u + 1)
                        nc.scalar.activation(e, e, ACT.Exp, scale=-1.0).then_inc(a_step, 1)
                        act.wait_ge(a_step, L * 2 * NU["A"] + 2 * u + 2)
                        nc.scalar.activation(e, e, ACT.Ln, bias=1.0).then_inc(l_done, 1)

                    def stick_weights(u):
                        n = key_tiles("A", u) * P
                        act.wait_ge(d_done, L * NU["A"] + u + 1)
                        if u >= 2:
                            act.wait_ge(t_done["A"], L * NU["A"] + u - 1)
                        nc.scalar.activation(w_buf[:, u % 2, 0:n], c_buf[:, u % 2, 0:n],
                                             ACT.Exp).then_inc(w_done["A"], 1)

                    softplus_part(0)
                    for u in range(NU["A"] + 2):
                        if u >= 2 and u % 2 == 0:
                            move_T("A", L, u - 2)
                        if 1 <= u <= NU["A"]:
                            stick_weights(u - 1)
                        if u + 1 < NU["A"]:
                            softplus_part(u + 1)

                    for i in range(0, 8, 2):
                        act.wait_ge(tb_tr, L * 10 + i + 1)
                        nc.scalar.activation(qT_B[:, i // 2, 0:HALF], B(i), ACT.Copy,
                                             scale=SCALE_A).then_inc(tb_act, 1)
                    for i in range(2):
                        act.wait_ge(tb_tr, L * 10 + 9 + i)
                        at = HD + i * HALF
                        nc.scalar.activation(kT_B[:, at:at + HALF], B(i), ACT.Copy).then_inc(tb_act, 1)

                    def window_weights(u):
                        act.wait_ge(top_done, L * NT + u + 1)
                        if u >= 2:
                            act.wait_ge(t_done["B"], L * NU["B"] + u - 1)
                        nc.scalar.activation(psm[:, u, :], top[:, u % 2, :], ACT.Exp).then_inc(es_done, 1)
                        for m in range(B_HEADS):
                            last = nc.scalar.activation(w_buf[:, u % 2, m * P:(m + 1) * P],
                                                        pair(u % 2)[:, m * P:(m + 1) * P], ACT.Exp,
                                                        bias=ntop[:, u % 2, m:m + 1],
                                                        accum_out=rden[:, u, m:m + 1])
                        last.then_inc(w_done["B"], 1)

                    for u in range(NU["B"] + 2):
                        if u >= 2 and u % 2 == 0:
                            move_T("B", L, u - 2)
                        if u < NU["B"]:
                            window_weights(u)

                    act.wait_ge(o_done["B"], (L + 1) * NU["B"])
                    for t in range(NT):
                        nc.scalar.activation(junk_q[:, t, :], p[:, t, CQ:CQ + Q_RANK], ACT.Square,
                                             scale=Q_RANK ** -0.5, accum_out=gms[:, 0, t:t + 1])
                        nc.scalar.activation(junk_kv[:, t, :], p[:, t, CKV:CKV + KV_RANK], ACT.Square,
                                             scale=KV_RANK ** -0.5, accum_out=gms[:, 1, t:t + 1]).then_inc(tc_sq, 1)
                    for i in range(0, 6, 2):
                        act.wait_ge(tc_tr, L * 6 + i + 1)
                        dst = (cqT[:, i // 2, 0:HALF] if i < 4 else ckvT[:, 0:HALF])
                        nc.scalar.activation(dst, B(i), ACT.Copy).then_inc(tc_act, 1)
                    for t in range(NT + 1):
                        if t < NT:
                            b0 = 2 * (t % 2)
                            act.wait_ge(up_done, L * 2 * NT + 2 * t + 1)
                            if t >= 2:
                                act.wait_ge(asm_tr, L * 2 * NT + 2 * (t - 1))
                            nc.scalar.activation(
                                qk_asm[:, t % 2, 0, :, 0:HD],
                                B(b0)[:, 0:C_HEADS * QK_C].rearrange("p (h d) -> p h d", d=QK_C)[:, :, 0:HD],
                                ACT.Copy).then_inc(up_act, 1)
                            act.wait_ge(up_done, L * 2 * NT + 2 * t + 2)
                            kv = B(b0 + 1).rearrange("p (h d) -> p h d", d=2 * HD)
                            nc.scalar.activation(qk_asm[:, t % 2, 1, :, 0:HD], kv[:, :, 0:HD],
                                                 ACT.Copy).then_inc(up_act, 1)
                            nc.scalar.activation(p[:, t, VA:VA + C_HEADS * HD].rearrange("p (h d) -> p h d", d=HD),
                                                 kv[:, :, HD:2 * HD], ACT.Copy).then_inc(up_act, 1)
                        if t >= 1:
                            act.wait_ge(asm_tr, L * 2 * NT + 2 * (t - 1) + 1)
                            nc.scalar.activation(qT_C[0:QK_C, :, (t - 1) * P:t * P],
                                                 B(4)[0:QK_C, :].rearrange("p (h n) -> p h n", h=C_HEADS),
                                                 ACT.Copy).then_inc(asm_act, 1)

                    def latent_weights(u):
                        h, b = units["C"][u]
                        n = (b + 1) * P
                        act.wait_ge(topc_done, L * NU["C"] + u + 1)
                        if u >= 2:
                            act.wait_ge(t_done["C"], L * NU["C"] + u - 1)
                        nc.scalar.activation(w_buf[:, u % 2, 0:n], pair(u % 2)[:, 0:n], ACT.Exp,
                                             bias=ntop[:, u % 2, 0:1], scale=SCALE_C,
                                             accum_out=psm[:, b, h:h + 1]).then_inc(w_done["C"], 1)

                    for u in range(NU["C"] + 2):
                        if u >= 2 and u % 2 == 0:
                            move_T("C", L, u - 2)
                        if u < NU["C"]:
                            latent_weights(u)

                    act.wait_ge(o_done["C"], (L + 1) * NU["C"])
                    for t in range(NT):
                        for g, (at, width, to) in enumerate(((QA, 256, 0), (QB, 512, 256), (OC, 256, 768))):
                            last = nc.scalar.activation(junk_g[:, t, to:to + width], p[:, t, at:at + width],
                                                        ACT.Square, scale=width ** -0.5,
                                                        accum_out=gms[:, g, t:t + 1])
                        last.then_inc(g_sq, 1)
                    for q in range(2 * NT):
                        t, j = q // 2, q % 2
                        act.wait_ge(oT_tr, L * 2 * NT + q + 1)
                        nc.scalar.activation(hT_hi[:, 4 * j:4 * j + 4, t * P:(t + 1) * P],
                                             B(4 + q % 4).rearrange("p (k n) -> p k n", k=4),
                                             ACT.Copy).then_inc(oT_hi, 1)

                    norm(2 * L + 1, lambda t: act.wait_ge(wadd_done, L * 2 * NT + NT + t + 1))

                    def relu(G0, first):
                        act.wait_ge(mu_done, G0 + (first + 1))
                        if first >= 2:
                            act.wait_ge(msq_done, G0 + (first - 1))
                        nc.scalar.activation(relu_t[:, first % 2, :], B(first % 4), ACT.Relu).then_inc(relu_done, 1)

                    def high(G0, first):
                        act.wait_ge(msq_done, G0 + (first + 1))
                        s = first % 8
                        nc.scalar.activation(aT_hi[:, s // 2, (s % 2) * HALF:(s % 2 + 1) * HALF], B(first % 4),
                                             ACT.Copy).then_inc(mhi_done, 1)

                    def groups(G0, first):
                        for g in range(4):
                            relu(G0, first + g)
                            if g >= 1:
                                high(G0, first + g - 1)
                        high(G0, first + 3)

                    groups(L * 4 * NC, 0)
                    groups(L * 4 * NC, 4)
                    with act_engine.Fori(0, NC // 2 - 1) as i_reg:
                        i = Count(0, [(i_reg, 1)])
                        groups(L * 4 * NC + 8 * i, 8)
                        groups(L * 4 * NC + 8 * i, 12)

                with act_engine.Fori(0, depth) as L:
                    layer(L, Count(0, [(L, 1)]))

                for t in range(NT):
                    act.wait_ge(madd_done, depth * 16 * NC)
                    if t >= 2:
                        act.wait_ge(stored[t % 2], 16 * (t // 2))
                    nc.scalar.activation(hn[:, t % 2, :], x[:, t, :], ACT.Square, scale=D ** -0.5,
                                         accum_out=ms[:, t:t + 1]).then_inc(sq_done, 1)

            @block.vector
            def _(dve_engine):
                dve = Waiter(dve_engine, "dve")
                chain = [0]
                DVE_LINKS = 2 * NU["A"] + 2 + 4 * NT + 2 * NU["C"]


                def link(ins, L):
                    chain[0] += 1
                    ins.then_inc(dve_chain, 1)
                    dve.wait_ge(dve_chain, L * DVE_LINKS + chain[0])

                def norm_row(L2, t, gains):
                    dve.wait_ge(rstd_done, L2 * NT + t + 1)
                    if t == 0:
                        dve.wait_ge(gain_loaded, gains)
                    nc.vector.scalar_tensor_tensor(hn[:, t % 2, :], x[:, t, :], rs[:, t:t + 1], gain[:, 0:D],
                                                   ALU.mult, ALU.mult).then_inc(hn_done, 1)

                def hT_low(L2, t):
                    for j in range(2):
                        q = 2 * t + j
                        dve.wait_ge(hT_hi_done, L2 * 2 * NT + q + 1)
                        dst = slice(t * P, (t + 1) * P)
                        nc.vector.tensor_tensor(hT_lo[:, 4 * j:4 * j + 4, dst],
                                                B(4 + q % 4).rearrange("p (k n) -> p k n", k=4),
                                                hT_hi[:, 4 * j:4 * j + 4, dst].bitcast(F32),
                                                ALU.subtract).then_inc(hT_lo_done, 1)

                def move_T(g, L, u):
                    dve.wait_ge(t_done[g], L * NU[g] + u + 1)
                    n = key_tiles(g, u) * P
                    nc.vector.tensor_copy(wT[:, u % 2, 0:n], pair(2)[:, 0:n]).then_inc(te_dve[g], 1)

                def layer(L_reg, L):
                    chain[0] = 0
                    for t in range(NT):
                        norm_row(2 * L, t, L * 80 + 16)
                        if t >= 1:
                            hT_low(2 * L, t - 1)
                    hT_low(2 * L, NT - 1)

                    for j in range(4):
                        for t in range(1, NT, 2):
                            dve.wait_ge(proj_done, L * 4 * NT + NT * j + t + 1)
                            nc.vector.tensor_copy(p[:, t, j * HALF:j * HALF + BLOCKS[j]],
                                                  B(t)[:, 0:BLOCKS[j]]).then_inc(p_dve, 1)

                    for i in range(1, 8, 2):
                        dve.wait_ge(ta_tr, L * 8 + i + 1)
                        dst = (qT_A if i < 4 else kT_A)[:, (i // 2) % 2, HALF:S]
                        nc.vector.tensor_scalar(dst, B(i), SCALE_A if i < 4 else 1.0, None,
                                                ALU.mult).then_inc(ta_dve, 1)

                    def stick_sums(u):
                        n = key_tiles("A", u) * P
                        z, e, c = pair(u % 2)[:, 0:n], e_buf[:, u % 2, 0:n], c_buf[:, u % 2, 0:n]
                        dve.wait_ge(l_done, L * NU["A"] + u + 1)
                        if u >= 2:
                            dve.wait_ge(w_done["A"], L * NU["A"] + u - 1)
                        link(nc.vector.scalar_tensor_tensor(c, z, 0.0, e, ALU.max, ALU.add), L)
                        link(nc.vector.tensor_tensor_scan(e[:, ::-1], c[:, ::-1], c[:, ::-1], 0.0,
                                                          ALU.add, ALU.bypass), L)
                        nc.vector.tensor_tensor(c, z, e, ALU.subtract).then_inc(d_done, 1)

                    def out_A(u):
                        h, b = units["A"][u]
                        dve.wait_ge(pv_done["A"], L * NU["A"] + u + 1)
                        nc.vector.tensor_copy(p[:, b, QA + h * HD:QA + (h + 1) * HD],
                                              B(6 + u % 2)[:, 0:HD]).then_inc(o_done["A"], 1)

                    for u in range(NU["A"] + 3):
                        if 2 <= u < NU["A"] + 2 and u % 2 == 1:
                            move_T("A", L, u - 2)
                        if u >= 3:
                            out_A(u - 3)
                        if u < NU["A"]:
                            stick_sums(u)

                    for i in range(1, 8, 2):
                        dve.wait_ge(tb_tr, L * 10 + i + 1)
                        nc.vector.tensor_scalar(qT_B[:, i // 2, HALF:S], B(i), SCALE_A, None,
                                                ALU.mult).then_inc(tb_dve, 1)
                    nc.vector.memset(kT_B[:, 0:HD], 0.0).then_inc(tb_fill, 1)
                    nc.vector.memset(kT_Bs[:, 0:HD], 0.0).then_inc(tb_fill, 1)
                    nc.vector.memset(v_Bs[0:HD, 0, :], 0.0).then_inc(tb_fill, 1)
                    nc.vector.tensor_copy(v_Bs[0:HD, 1:NT, :], p[HD:P, 0:NT - 1, VB:VB + P]).then_inc(tb_fill, 1)
                    nc.vector.tensor_copy(v_Bs[HD:P, :, :], p[0:HD, :, VB:VB + P]).then_inc(tb_fill, 1)
                    for i in range(2):
                        dve.wait_ge(tb_act, L * 6 + 5 + i)
                        at = HD + i * HALF
                        nc.vector.tensor_copy(kT_Bs[0:HD, at:at + HALF], B(i)[HD:P, :]).then_inc(tb_fill, 1)
                        nc.vector.tensor_copy(kT_Bs[HD:P, at:at + HALF], B(i)[0:HD, :]).then_inc(tb_fill, 1)
                    dve.wait_ge(sink_loaded, L * 32 + 32)
                    link(nc.vector.tensor_scalar(nsink[:, :], sink[:, :], -1.0, None, ALU.mult), L)

                    def window_top(u):
                        s = pair(u % 2).rearrange("p (h n) -> p h n", h=B_HEADS)
                        dve.wait_ge(z_done["B"], L * NU["B"] + u + 1)
                        if u == 0:
                            link(nc.vector.memset(s[0:HD, :, 0:HD], BIG), L)
                        link(nc.vector.tensor_reduce(ntop[:, u % 2, :], s, AX_X, ALU.max, negate=True), L)
                        link(nc.vector.tensor_tensor(ntop[:, u % 2, :], ntop[:, u % 2, :], nsink[:, :], ALU.min), L)
                        if u >= 2:
                            dve.wait_ge(es_done, L * NT + u - 1)
                        nc.vector.tensor_tensor(top[:, u % 2, :], ntop[:, u % 2, :], sink[:, :],
                                                ALU.add).then_inc(top_done, 1)

                    def out_B(u):
                        dve.wait_ge(w_done["B"], L * NU["B"] + u + 1)
                        link(nc.vector.tensor_tensor(rden[:, u, :], rden[:, u, :], psm[:, u, :],
                                                     ALU.add), L)
                        link(nc.vector.reciprocal(rden[:, u, :], rden[:, u, :]), L)
                        dve.wait_ge(pv_done["B"], L * NU["B"] + u + 1)
                        r = rden[:, u, :].rearrange("p (e h) -> p h e", e=2).unsqueeze(3)
                        nc.vector.tensor_tensor(
                            p[:, u, QB:KB].rearrange("p (h e d) -> p h e d", e=2, d=HD),
                            B(6 + u % 2).rearrange("p (h e d) -> p h e d", e=2, d=HD),
                            r.to_broadcast([P, 4, 2, HD]), ALU.mult).then_inc(o_done["B"], 1)

                    window_top(0)
                    for u in range(NU["B"] + 3):
                        if 2 <= u < NU["B"] + 2 and u % 2 == 1:
                            move_T("B", L, u - 2)
                        if u >= 3:
                            out_B(u - 3)
                        if u + 1 < NU["B"]:
                            window_top(u + 1)

                    dve.wait_ge(tc_rs, L + 1)
                    dve.wait_ge(gain_loaded, L * 80 + 48)
                    for t in range(NT):
                        for at, to, width, r in ((CQ, 0, Q_RANK, 0), (CKV, Q_RANK, KV_RANK, 1)):
                            v = p[:, t, at:at + width]
                            nc.vector.scalar_tensor_tensor(v, v, grs[:, r, t:t + 1], gain[:, to:to + width],
                                                           ALU.mult, ALU.mult).then_inc(tc_n, 1)
                    for i in range(1, 6, 2):
                        dve.wait_ge(tc_tr, L * 6 + i + 1)
                        dst = (cqT[:, i // 2, HALF:S] if i < 4 else ckvT[:, HALF:S])
                        nc.vector.tensor_copy(dst, B(i)).then_inc(tc_dve, 1)
                    dve.wait_ge(rope_step, (L + 1) * 8 * NT)
                    for t in range(NT + 1):
                        if t < NT:
                            b0 = 2 * (t % 2)
                            if t >= 2:
                                dve.wait_ge(asm_tr, L * 2 * NT + 2 * (t - 1))
                            dve.wait_ge(up_act, L * 3 * NT + 3 * t + 3)
                            q = B(b0)[:, 0:C_HEADS * QK_C].rearrange("p (h d) -> p h d", d=QK_C)[:, :, HD:QK_C]
                            cos, sin = (rope_c[:, t, a:a + 1, :] for a in range(2))
                            m1, m2 = rope_t[:, t % 2, 0, :, :], rope_t[:, t % 2, 1, :, :]
                            hf = ROPE_C // 2
                            nc.vector.tensor_tensor(m1, q, cos.to_broadcast([P, C_HEADS, ROPE_C]),
                                                    ALU.mult).then_inc(up_dve, 1)
                            for a in range(2):
                                nc.vector.tensor_tensor(
                                    m2[:, :, a * hf:(a + 1) * hf], q[:, :, (1 - a) * hf:(2 - a) * hf],
                                    sin[:, :, a * hf:(a + 1) * hf].to_broadcast([P, C_HEADS, hf]),
                                    ALU.mult).then_inc(up_dve, 1)
                            dve.wait_ge(up_dve, L * 5 * NT + 5 * t + 3)
                            nc.vector.tensor_tensor(qk_asm[:, t % 2, 0, :, HD:QK_C], m1, m2,
                                                    ALU.add).then_inc(up_dve, 1)
                            nc.vector.tensor_copy(
                                qk_asm[:, t % 2, 1, :, HD:QK_C],
                                p[:, t, KR:IN_W].unsqueeze(1).to_broadcast([P, C_HEADS, ROPE_C])).then_inc(up_dve, 1)
                        if t >= 1:
                            dve.wait_ge(asm_tr, L * 2 * NT + 2 * (t - 1) + 2)
                            nc.vector.tensor_copy(kT_C[0:QK_C, :, (t - 1) * P:t * P],
                                                  B(5)[0:QK_C, :].rearrange("p (h n) -> p h n", h=C_HEADS)
                                                  ).then_inc(asm_dve, 1)

                    def latent_top(u):
                        n = key_tiles("C", u) * P
                        dve.wait_ge(z_done["C"], L * NU["C"] + u + 1)
                        link(nc.vector.tensor_reduce(top[:, u % 2, 0:1], pair(u % 2)[:, 0:n], AX_X, ALU.max), L)
                        nc.vector.tensor_scalar(ntop[:, u % 2, 0:1], top[:, u % 2, 0:1], -SCALE_C, None,
                                                ALU.mult).then_inc(topc_done, 1)

                    def out_C(u):
                        h, b = units["C"][u]
                        dve.wait_ge(w_done["C"], L * NU["C"] + u + 1)
                        link(nc.vector.reciprocal(rden[:, b, h:h + 1], psm[:, b, h:h + 1]), L)
                        dve.wait_ge(pv_done["C"], L * NU["C"] + u + 1)
                        nc.vector.tensor_scalar(p[:, b, OC + h * HD:OC + (h + 1) * HD], B(6 + u % 2)[:, 0:HD],
                                                rden[:, b, h:h + 1], None, ALU.mult).then_inc(o_done["C"], 1)

                    latent_top(0)
                    for u in range(NU["C"] + 3):
                        if 2 <= u < NU["C"] + 2 and u % 2 == 1:
                            move_T("C", L, u - 2)
                        if u >= 3:
                            out_C(u - 3)
                        if u + 1 < NU["C"]:
                            latent_top(u + 1)

                    dve.wait_ge(g_rs, L + 1)
                    for t in range(NT):
                        if t == 0:
                            dve.wait_ge(gain_loaded, L * 80 + 64)
                        for g, (at, width, to) in enumerate(((QA, 256, 0), (QB, 512, 256), (OC, 256, 768))):
                            v = p[:, t, at:at + width]
                            nc.vector.scalar_tensor_tensor(v, v, grs[:, g, t:t + 1], gain[:, to:to + width],
                                                           ALU.mult, ALU.mult).then_inc(g_n, 1)
                        if t >= 1:
                            oT_low(L, t - 1)
                    oT_low(L, NT - 1)

                    for m in range(2 * NT):
                        half, t = m // NT, m % NT
                        dve.wait_ge(wo_done, L * 2 * NT + m + 1)
                        xs = x[:, t, half * HALF:(half + 1) * HALF]
                        nc.vector.tensor_tensor(xs, B(m % 4), xs, ALU.add).then_inc(wadd_done, 1)
                        if half == 1:
                            dve.wait_ge(wadd_done, L * 2 * NT + m + 1)
                            norm_row(2 * L + 1, t, L * 80 + 80)
                            if t >= 1:
                                hT_low(2 * L + 1, t - 1)
                    hT_low(2 * L + 1, NT - 1)

                    def square(G0, first):
                        dve.wait_ge(relu_done, G0 + (first + 1))
                        nc.vector.scalar_tensor_tensor(B(first % 4), B(first % 4), 0.0, relu_t[:, first % 2, :],
                                                       ALU.max, ALU.mult).then_inc(msq_done, 1)

                    def low(G0, first):
                        dve.wait_ge(mhi_done, G0 + (first + 1))
                        s = first % 8
                        at = slice((s % 2) * HALF, (s % 2 + 1) * HALF)
                        nc.vector.tensor_tensor(aT_lo[:, s // 2, at], B(first % 4),
                                                aT_hi[:, s // 2, at].bitcast(F32),
                                                ALU.subtract).then_inc(mlo_done, 1)

                    def groups(G0, first):
                        for g in range(4):
                            square(G0, first + g)
                            if g >= 1:
                                low(G0, first + g - 1)
                        low(G0, first + 3)

                    def adds(M0, first):
                        for m in range(16):
                            t, half = m // 2, m % 2
                            dve.wait_ge(md_done, M0 + (first + m + 1))
                            if first:
                                dve.wait_ge(madd_done, M0 + (first + m - 15))
                            xs = x[:, t, half * HALF:(half + 1) * HALF]
                            nc.vector.tensor_tensor(xs, B(4 + m % 4), xs, ALU.add).then_inc(madd_done, 1)

                    G, M = L * 4 * NC, L * 16 * NC
                    groups(G, 0)
                    groups(G, 4)
                    adds(M, 0)
                    with dve_engine.Fori(0, NC // 2 - 1) as i_reg:
                        i = Count(0, [(i_reg, 1)])
                        groups(G + 8 * i, 8)
                        adds(M + 32 * i, 16)
                        groups(G + 8 * i, 12)
                        adds(M + 32 * i, 32)
                    adds(M, 16 * (NC - 1))
                    dve.wait_ge(madd_done, M + 16 * NC)
                    dve_engine.sem_inc(layer_ready, 1)
                    assert chain[0] == DVE_LINKS, chain[0]

                def oT_low(L, t):
                    for j in range(2):
                        q = 2 * t + j
                        dve.wait_ge(oT_hi, L * 2 * NT + q + 1)
                        dst = slice(t * P, (t + 1) * P)
                        nc.vector.tensor_tensor(hT_lo[:, 4 * j:4 * j + 4, dst],
                                                B(4 + q % 4).rearrange("p (k n) -> p k n", k=4),
                                                hT_hi[:, 4 * j:4 * j + 4, dst].bitcast(F32),
                                                ALU.subtract).then_inc(oT_lo, 1)

                dve.wait_ge(consts_in, 4 * 16)
                nc.vector.tensor_copy(identb[:, :], ident[:, :]).then_inc(masks_ready, 1)
                nc.vector.tensor_copy(causal[:, :], masks_in[:, 0, :]).then_inc(masks_ready, 1)
                nc.vector.tensor_copy(chunk[:, :], masks_in[:, 1, :]).then_inc(masks_ready, 1)
                dve_engine.sem_inc(layer_ready, 1)
                with dve_engine.Fori(0, depth) as L:
                    layer(L, Count(0, [(L, 1)]))
                for t in range(NT):
                    norm_row(2 * depth, t, depth * 80 + 16)

            @block.tensor
            def _(pe_engine):
                pe = Waiter(pe_engine, "pe")
                mm = nc.tensor.matmul

                def three(out_, a, b, first, last):
                    mm(out_, a[0], b[0], start=first, stop=False)
                    mm(out_, a[0], b[1], start=False, stop=False)
                    return mm(out_, a[1], b[0], start=False, stop=last)

                def hT(k, cols):
                    return hT_hi[:, k, cols], hT_lo[:, k, cols]

                def turn_rows(done, src, q, k0):
                    for k in range(4):
                        last = nc.tensor.transpose(B(4 + q % 4)[:, k * P:(k + 1) * P], src(k0 + k), ident[:, :])
                    last.then_inc(done, 1)

                def norm_turn(L2, t):
                    pe.wait_ge(hn_done, L2 * NT + t + 1)
                    for j in range(2):
                        q = 2 * t + j
                        if q >= 4:
                            pe.wait_ge(hT_lo_done, L2 * 2 * NT + q - 3)
                        turn_rows(norm_tr, lambda k: hn[:, t % 2, k * P:(k + 1) * P], q, 4 * j)

                def layer(L_reg, L):
                    pe.wait_ge(layer_ready, L + 1)
                    for t in range(NT):
                        norm_turn(2 * L, t)

                    for j in range(4):
                        for i in range(4):
                            u = 4 * j + i
                            pe.wait_ge(split_done, L * U_ALL + u + 1)
                            for t in range(NT):
                                if u == 0:
                                    pe.wait_ge(hT_lo_done, 2 * L * 2 * NT + (2 * (t + 1) if t < 4 else 2 * NT))
                                if i == 0 and j > 0:
                                    pe.wait_ge(p_dve if t % 2 else p_act, L * 16 + 4 * (j - 1) + t // 2 + 1)
                                for kk in range(2):
                                    k = 2 * i + kk
                                    n = BLOCKS[j]
                                    wcol = slice(kk * n, (kk + 1) * n)
                                    s = slot_of[u]
                                    last = three(B(t)[:, 0:n], hT(k, slice(t * P, (t + 1) * P)),
                                                 (W(s)[:, wcol], W(s, True)[:, wcol]), k == 0, k == NK - 1)
                                if i == 3:
                                    last.then_inc(proj_done, 1)
                            if i < 3:
                                last.then_inc(in_used, 1)

                    pe.wait_ge(p_act, (L + 1) * 16)
                    pe.wait_ge(p_dve, (L + 1) * 16)
                    for i in range(8):
                        at = (QA if i < 4 else KA) + ((i // 2) % 2) * P
                        for tt in range(4):
                            t = 4 * (i % 2) + tt
                            last = nc.tensor.transpose(B(i)[:, tt * P:(tt + 1) * P], p[:, t, at:at + P], ident[:, :])
                        last.then_inc(ta_tr, 1)

                    def scores(g, u):
                        h, b = units[g][u]
                        z = pair(u % 2)
                        if g == "B":
                            for m in range(B_HEADS):
                                r = (m % 2) * HD
                                kT = kT_B if m % 2 == m // 4 else kT_Bs
                                for half in range(2):
                                    q0 = b * P + half * HD
                                    last = mm(z[half * HD:(half + 1) * HD, b_cols(m):b_cols(m) + P],
                                              qT_B[r:r + HD, m // 2, q0:q0 + HD], kT[r:r + HD, q0:q0 + P],
                                              start=True, stop=True)
                            last.then_inc(z_done[g], 1)
                            return
                        if g == "A":
                            r = (h % 2) * HD
                            q = qT_A[r:r + HD, h // 2, b * P:(b + 1) * P]
                            k = kT_A[r:r + HD, h // 2, :]
                            mask = causal
                        else:
                            q = qT_C[0:QK_C, h, b * P:(b + 1) * P]
                            k = kT_C[0:QK_C, h, :]
                            mask = chunk
                        n = (b + 1) * P
                        for c0 in range(0, n, HALF):
                            c1 = min(n, c0 + HALF)
                            mm(z[:, c0:c1], q, k[:, c0:c1], start=True, stop=c1 < n)
                        mm(z[:, b * P:n], identb[:, :], mask[:, :], start=False, stop=True).then_inc(z_done[g], 1)

                    def turn_weights(g, L, u):
                        pe.wait_ge(w_done[g], L * NU[g] + u + 1)
                        if u >= 1:
                            wait_moved(pe, g, L, u - 1)
                        for kb in range(key_tiles(g, u)):
                            last = nc.tensor.transpose(pair(2)[:, kb * P:(kb + 1) * P],
                                                       w_buf[:, u % 2, kb * P:(kb + 1) * P], ident[:, :])
                        last.then_inc(t_done[g], 1)

                    def weigh_values(g, L, u):
                        wait_moved(pe, g, L, u)
                        if u >= 2:
                            pe.wait_ge(o_done[g], L * NU[g] + u - 1)
                        h, b = units[g][u]
                        o = B(6 + u % 2)
                        if g == "B":
                            for m in range(B_HEADS):
                                v0 = (m // 4) * HD
                                for half in range(2):
                                    v = (p[:, b, VB + v0:VB + v0 + HD] if half else v_Bs[:, b, v0:v0 + HD])
                                    c0 = b_cols(m) + half * HD
                                    last = mm(o[half * HD:(half + 1) * HD, m * HD:(m + 1) * HD],
                                              wT[:, u % 2, c0:c0 + HD], v, start=True, stop=True)
                        else:
                            for kb in range(b + 1):
                                last = mm(o[:, 0:HD], wT[:, u % 2, kb * P:(kb + 1) * P],
                                          p[:, kb, VA + h * HD:VA + (h + 1) * HD], start=kb == 0, stop=kb == b)
                        last.then_inc(pv_done[g], 1)

                    def attend(g, z_free):
                        passed = pe_passed if g == "B" else None
                        scores(g, 0)
                        for u in range(NU[g]):
                            if u + 1 < NU[g]:
                                if u >= 1:
                                    pe.wait_ge(z_free[0], L * NU[g] + u, apart=passed)
                                scores(g, u + 1)
                            if u >= 1:
                                turn_weights(g, L, u - 1)
                            if u >= 2:
                                weigh_values(g, L, u - 2)
                        turn_weights(g, L, NU[g] - 1)
                        weigh_values(g, L, NU[g] - 2)
                        weigh_values(g, L, NU[g] - 1)

                    pe.wait_ge(ta_act, (L + 1) * 4)
                    pe.wait_ge(ta_dve, (L + 1) * 4)
                    attend("A", (d_done,))

                    pe.wait_ge(rope_step, (L + 1) * 8 * NT)
                    pe.wait_ge(o_done["A"], (L + 1) * NU["A"])
                    for i in range(10):
                        at = QB + (i // 2) * P
                        if i >= 8:
                            pe.wait_ge(tb_act if i == 8 else tb_dve, L * (6 if i == 8 else 4) + 1)
                        for tt in range(4):
                            t = 4 * (i % 2) + tt
                            last = nc.tensor.transpose(B(i % 8)[:, tt * P:(tt + 1) * P], p[:, t, at:at + P],
                                                       ident[:, :])
                        last.then_inc(tb_tr, 1)
                    pe.wait_ge(tb_act, (L + 1) * 6)
                    pe.wait_ge(tb_dve, (L + 1) * 4)
                    pe.wait_ge(tb_fill, (L + 1) * 9, apart=pe_passed)
                    attend("B", (w_done["B"],))

                    pe.wait_ge(o_done["B"], (L + 1) * NU["B"])
                    pe.wait_ge(tc_n, (L + 1) * 2 * NT)
                    for i in range(6):
                        at = CQ + (i // 2) * P
                        for tt in range(4):
                            t = 4 * (i % 2) + tt
                            last = nc.tensor.transpose(B(i)[:, tt * P:(tt + 1) * P], p[:, t, at:at + P], ident[:, :])
                        last.then_inc(tc_tr, 1)
                    pe.wait_ge(tc_act, (L + 1) * 3)
                    pe.wait_ge(tc_dve, (L + 1) * 3)
                    pe.wait_ge(up_loaded, (L + 1) * 32)
                    for t in range(NT + 1):
                        if t < NT:
                            b0 = 2 * (t % 2)
                            tok = slice(t * P, (t + 1) * P)
                            if t >= 2:
                                pe.wait_ge(up_act, L * 3 * NT + 3 * (t - 1))
                                pe.wait_ge(up_dve, L * 5 * NT + 5 * (t - 2) + 3)
                            for k in range(2):
                                last = mm(B(b0)[:, 0:C_HEADS * QK_C], cqT[:, k, tok], w_uq[:, k, :],
                                          start=k == 0, stop=k == 1)
                            last.then_inc(up_done, 1)
                            mm(B(b0 + 1), ckvT[:, tok], w_ukv[:, :], start=True, stop=True).then_inc(up_done, 1)
                        if t >= 1:
                            s = (t - 1) % 2
                            pe.wait_ge(up_act, L * 3 * NT + 3 * t)
                            pe.wait_ge(up_dve, L * 5 * NT + 5 * t)
                            if t >= 2:
                                pe.wait_ge(asm_act, L * NT + t - 1)
                                pe.wait_ge(asm_dve, L * NT + t - 1)
                            for a in range(2):
                                for h in range(C_HEADS):
                                    last = nc.tensor.transpose(B(4 + a)[0:QK_C, h * P:(h + 1) * P],
                                                               qk_asm[:, s, a, h, :], ident[:, :])
                                last.then_inc(asm_tr, 1)
                    pe.wait_ge(asm_act, (L + 1) * NT)
                    pe.wait_ge(asm_dve, (L + 1) * NT)
                    attend("C", (w_done["C"],))

                    for t in range(NT):
                        pe.wait_ge(g_n, L * 3 * NT + 3 * (t + 1))
                        for j in range(2):
                            q = 2 * t + j
                            if q >= 4:
                                pe.wait_ge(oT_lo, L * 2 * NT + q - 3)
                            cols = [QA, QA + P, QB, QB + P, QB + 2 * P, QB + 3 * P, OC, OC + P]
                            turn_rows(oT_tr, lambda k: p[:, t, cols[k]:cols[k] + P], q, 4 * j)

                    for m in range(2 * NT):
                        half, t = m // NT, m % NT
                        pe.wait_ge(oT_lo, L * 2 * NT + 2 * (t + 1))
                        if m >= 4:
                            pe.wait_ge(wadd_done, L * 2 * NT + m - 3)
                        for k in range(NK):
                            u = U_IN + 4 * half + k // 2
                            if t == 0 and k % 2 == 0:
                                pe.wait_ge(split_done, L * U_ALL + u + 1)
                            s = slot_of[u]
                            wcol = slice((k % 2) * HALF, (k % 2 + 1) * HALF)
                            last = three(B(m % 4), hT(k, slice(t * P, (t + 1) * P)),
                                         (W(s)[:, wcol], W(s, True)[:, wcol]), k == 0, k == NK - 1)
                        last.then_inc(wo_done, 1)
                        if half == 1 and t >= 1:
                            norm_turn(2 * L + 1, t - 1)
                    norm_turn(2 * L + 1, NT - 1)

                    def up(G0, first, c_parity, U0, ufirst):
                        for g in range(4):
                            f, half = g // 2, g % 2
                            if g % 2 == 0:
                                pe.wait_ge(split_done, U0 + (ufirst + f + 1))
                            if first:
                                pe.wait_ge(mlo_done, G0 + (first + g - 3))
                            else:
                                pe.wait_ge(hT_lo_done, (2 * L + 1) * 2 * NT + (NT if g == 0 else 2 * NT))
                            s = 4 * c_parity + f
                            for k in range(NK):
                                wc = slice(k * P, (k + 1) * P)
                                last = three(B(g), (W(s)[:, wc], W(s, True)[:, wc]),
                                             hT(k, slice(half * HALF, (half + 1) * HALF)), k == 0, k == NK - 1)
                            last.then_inc(mu_done, 1)

                    def down(M0, first, c_parity, G0, gfirst, U0, ufirst):
                        pe.wait_ge(mlo_done, G0 + (gfirst + 4))
                        pe.wait_ge(split_done, U0 + (ufirst + 2))
                        for m in range(16):
                            t, half = m // 2, m % 2
                            if first or m >= 4:
                                pe.wait_ge(madd_done, M0 + (first + m - 3))
                            for f in range(2):
                                s = 4 * c_parity + 2 + f
                                a = 2 * c_parity + f
                                tok = slice(t * P, (t + 1) * P)
                                cols = slice(half * HALF, (half + 1) * HALF)
                                last = three(B(4 + m % 4), (aT_hi[:, a, tok], aT_lo[:, a, tok]),
                                             (W(s)[:, cols], W(s, True)[:, cols]), f == 0, f == 1)
                            last.then_inc(md_done, 1)

                    G, M, U = L * 4 * NC, L * 16 * NC, L * U_ALL
                    up(G, 0, 0, U, U_M)
                    up(G, 4, 1, U, U_M + 2)
                    down(M, 0, 0, G, 0, U, U_M + 4)
                    with pe_engine.Fori(0, NC // 2 - 1) as i_reg:
                        i = Count(0, [(i_reg, 1)])
                        Gi, Mi, Ui = G + 8 * i, M + 32 * i, U + 8 * i
                        for k in range(2):
                            up(Gi, 8 + 4 * k, k, Ui, U_M + 6 + 4 * k)
                            down(Mi, 16 * (k + 1), 1 - k, Gi, 4 * (k + 1), Ui, U_M + 8 + 4 * k)
                    down(M, 16 * (NC - 1), 1, G, 4 * (NC - 1), U, U_ALL - 2)

                pe.wait_ge(consts_in, 4 * 16)
                pe.wait_ge(masks_ready, 3)
                with pe_engine.Fori(0, depth) as L:
                    layer(L, Count(0, [(L, 1)]))


_INS = ["x", "attn_norm", "w_in", "mla_q_norm", "mla_kv_norm", "w_mla_uq", "w_mla_ukv", "sink_logits",
        "group_norm", "w_out", "mlp_norm", "w_mlp_in", "w_mlp_out", "final_norm"]


def shape_constants():
    import numpy as np

    at = np.arange(P)
    causal = np.where(at[None, :] < at[:, None], 0.0, BIG).astype(np.float32)
    chunk = np.where(at[None, :] // HD <= at[:, None] // HD, 0.0, BIG).astype(np.float32)

    def rope(dim):
        inv = (np.float32(1.0) / np.float32(10000.0) ** (np.arange(0, dim, 2, dtype=np.float32) / np.float32(dim)))
        ang = np.arange(S, dtype=np.float32)[:, None] * inv.astype(np.float32)[None, :]
        cos, sin = np.cos(ang).astype(np.float32), np.sin(ang).astype(np.float32)
        tab = np.stack([np.concatenate([cos, cos], 1), np.concatenate([-sin, sin], 1)], 1)
        return np.ascontiguousarray(tab.reshape(NT, P, 2, dim).transpose(1, 0, 2, 3))

    return {"ident": np.eye(P, dtype=np.float32), "causal": causal,
            "chunk": chunk, "rope_b": rope(HD), "rope_c": rope(ROPE_C)}


def kernel(**inputs):
    import numpy as np
    import concourse.bacc as bacc
    from concourse.bass_utils import run_bass_kernel_spmd

    nc = bacc.Bacc("TRN2", target_bir_lowering=False, num_devices=1)
    arrays, args = {}, []
    given = {name: np.ascontiguousarray(inputs[name]) for name in _INS}
    for name, a in {**given, **shape_constants()}.items():
        arrays[f"in_{name}"] = a
        args.append(nc.dram_tensor(f"in_{name}", a.shape, mybir.dt.from_np(a.dtype), kind="ExternalInput").ap())
    args.append(nc.dram_tensor("out", (1, S, D), F32, kind="ExternalOutput").ap())
    hybrid_trunk(nc, *args)
    r = run_bass_kernel_spmd(nc, [arrays], core_ids=[0])
    return r.results[0]["out"]
```

```python
from contextlib import ExitStack

import concourse.bass as bass
from concourse import mybir

F32 = mybir.dt.float32
F32R = mybir.dt.float32r
BF16 = mybir.dt.bfloat16
ALU = mybir.AluOpType
ACT = mybir.ActivationFunctionType
AX_X = mybir.AxisListType.X

P = 128
D = 1024
S = 1024
DEPTH = 2
NT = S // P
NK = D // P
HALF = 512
HD = 64
EPS = 1e-6
BIG = -1e30

A_HEADS, B_HEADS, C_HEADS = 4, 8, 4
ROPE_C = 32
QK_C = HD + ROPE_C
Q_RANK, KV_RANK = 256, 128
QA, KA, VA = 0, 256, 512
QB, KB, VB = 768, 1280, 1408
CQ, CKV, KR = 1536, 1792, 1920
IN_W = 1952
OC = CQ

BLOCKS = [HALF, HALF, HALF, IN_W - 3 * HALF]
D_FF = 4096
NF = D_FF // P
NC = NF // 2

U_IN, U_OUT, U_MLP = 16, 8, 2 * NF
U_ALL = U_IN + U_OUT + U_MLP
U_M = U_IN + U_OUT

SCALE_A = HD ** -0.5
SCALE_C = QK_C ** -0.5


class Count:

    def __init__(self, const=0, terms=()):
        self.const, self.terms = const, tuple(terms)

    def __add__(self, other):
        if isinstance(other, Count):
            return Count(self.const + other.const, self.terms + other.terms)
        return Count(self.const + other, self.terms)

    __radd__ = __add__

    def __sub__(self, other):
        return self + (-other)

    def __mul__(self, by):
        return Count(self.const * by, [(var, k * by) for var, k in self.terms])

    __rmul__ = __mul__


class Waiter:

    def __init__(self, eng, name, apart=None):
        self.eng, self.name, self.regs, self.apart = eng, name, None, apart

    def wait_ge(self, semaphore, count, apart=None):
        if not isinstance(count, Count):
            return self.eng.wait_ge(semaphore, count)
        if self.regs is None:
            self.regs = [self.eng.alloc_register(f"{self.name}_{what}") for what in ("total", "part", "count")]
        total, part, reached = self.regs
        for n, (var, k) in enumerate(count.terms):
            self.eng.reg_mul(part if n else total, var, k)
            if n:
                self.eng.reg_add(total, total, part)
        assert count.const > 0, "a wait on a register's value is never on zero"
        self.eng.reg_add(reached, total, count.const)
        self.eng.wait_ge(semaphore, reached)
        apart = apart or self.apart
        if apart:
            self.eng.sem_inc(apart, 1)


def hybrid_trunk(nc, x_in, attn_norm, w_in, mla_q_norm, mla_kv_norm, w_mla_uq, w_mla_ukv, sink_logits,
                 group_norm, w_out, mlp_norm, w_mlp_in, w_mlp_out, final_norm,
                 ident_in, causal_in, chunk_in, rope_b_in, rope_c_in, out, depth=DEPTH):
    ctx = ExitStack()
    with ctx:
        start = (nc.sbuf_base + 127) // 128 * 128
        arena = {"at": start}

        def region(size):
            at = arena["at"]
            arena["at"] += size
            return at

        X, HT, PR, WA, RAW, CO = (region(k * 1024) for k in (32, 64, 64, 32, 8, 0))

        def place(name, shape, dt, offset):
            return nc.alloc_sbuf_tensor_at(name, shape, dt, offset=offset)

        KB_ = 1024
        x = place("x", [P, NT, D], F32, X)
        hT_hi = place("hT_hi", [P, NK, S], F32R, HT)
        hT_lo = place("hT_lo", [P, NK, S], F32R, HT + 32 * KB_)
        p = place("p", [P, NT, IN_W], F32, PR)
        ws_hi = [place("wsa_hi", [P, 4, 1024], F32R, WA), place("wsb_hi", [P, 4, 1024], F32R, PR)]
        ws_lo = [place("wsa_lo", [P, 4, 1024], F32R, WA + 16 * KB_),
                 place("wsb_lo", [P, 4, 1024], F32R, PR + 16 * KB_)]
        aT_hi = place("aT_hi", [P, 4, S], F32R, PR + 32 * KB_)
        aT_lo = place("aT_lo", [P, 4, S], F32R, PR + 48 * KB_)
        hn = place("hn", [P, 2, D], F32, PR + 48 * KB_)
        raw = place("raw", [P, 2, 1024], F32, RAW)

        e_buf = place("e_buf", [P, 2, S], F32, HT)
        c_buf = place("c_buf", [P, 2, S], F32, HT + 8 * KB_)
        w_buf = place("w_buf", [P, 2, S], F32, HT + 16 * KB_)
        wT = place("wT", [P, 2, S], F32, HT + 24 * KB_)
        cqT = place("cqT", [P, 2, S], F32, HT)
        ckvT = place("ckvT", [P, S], F32, HT + 8 * KB_)
        w_ukv = place("w_ukv", [P, HALF], F32, HT + 12 * KB_)
        qk_asm = place("qk_asm", [P, 2, 2, C_HEADS, QK_C], F32, HT + 16 * KB_)
        rope_t = place("rope_t", [P, 2, 2, C_HEADS, ROPE_C], F32, HT + 22 * KB_)
        w_uq = [place("w_uq0", [P, C_HEADS * QK_C], F32, HT + 14 * KB_),
                place("w_uq1", [P, C_HEADS * QK_C], F32, CO + 4 * (Q_RANK + KV_RANK))]
        squares = place("squares", [P, 2, HALF], F32, HT)
        masks_in = place("masks_in", [P, 2, P], F32, HT)
        qT_A = [place("qT_A0", [P, 2, S], F32, HT + 32 * KB_), place("qT_A1", [P, 2, S], F32, HT + 56 * KB_)]
        kT_A = place("kT_A", [P, 2, S], F32, HT + 40 * KB_)
        qT_B = place("qT_B", [P, 4, S], F32, HT + 32 * KB_)
        kT_C = place("kT_C", [P, C_HEADS, S], F32, HT + 32 * KB_)
        rope_b = place("rope_b", [P, NT, 2, HD], F32, HT + 48 * KB_)
        turned = place("turned", [P, 10, HD], F32, HT + 52 * KB_)
        KPAD = HD + S
        kT_B = place("kT_B", [P, KPAD], F32, HT + 48 * KB_)
        kT_Bs = place("kT_Bs", [P, KPAD], F32, HT + 48 * KB_ + 4 * KPAD)
        v_Bs = place("v_Bs", [P, NT, P], F32, HT + 48 * KB_ + 8 * KPAD)
        qT_C = place("qT_C", [P, C_HEADS, S], F32, HT + 48 * KB_)

        def const(name, shape, dt):
            size = 2 if dt == BF16 else 4
            for n in shape[1:]:
                size *= n
            at = region((size + 31) // 32 * 32)
            assert at + size <= nc.sbuf_usable_end, (name, at + size - nc.sbuf_usable_end)
            return place(name, shape, dt, at)

        gain = const("gain", [P, 1024], F32)
        relu_t = place("relu_t", [P, 2, HALF], F32, CO)
        ident = const("ident", [P, P], F32)
        identb = const("identb", [P, P], BF16)
        causal = const("causal", [P, P], BF16)
        chunk = const("chunk", [P, P], BF16)
        rope_c = const("rope_c", [P, NT, 2, ROPE_C], F32)
        sink = const("sink", [P, B_HEADS], F32)
        nsink = const("nsink", [P, B_HEADS], F32)
        ms = const("ms", [P, NT], F32)
        rs = const("rs", [P, NT], F32)
        gms = const("gms", [P, 5, NT], F32)
        grs = const("grs", [P, 5, NT], F32)
        power = const("power", [P, 1, NT], F32)
        top = const("top", [P, 2, B_HEADS], F32)
        ntop = const("ntop", [P, 2, B_HEADS], F32)
        psm = place("psm", [P, NT, B_HEADS], F32, PR + NT * IN_W * 4)
        rden = place("rden", [P, NT, B_HEADS], F32, PR + NT * IN_W * 4 + NT * B_HEADS * 4)

        bank = [ctx.enter_context(nc.psum_tensor(f"bank{i}", [P, 2, HALF], F32)) for i in range(4)]

        def B(i):
            return bank[i // 2][:, i % 2, :]

        def pair(i):
            return bank[i][:, :, :].rearrange("p a n -> p (a n)")

        def sem(name):
            return ctx.enter_context(nc.semaphore(name))

        consts_in, masks_ready = sem("consts_in"), sem("masks_ready")
        x_loaded = [sem(f"x_loaded{t}") for t in range(NT)]
        raw_loaded = [sem("raw_loaded0"), sem("raw_loaded1")]
        gain_loaded, sink_loaded, tab_loaded, up_loaded = (sem(n) for n in (
            "gain_loaded", "sink_loaded", "tab_loaded", "up_loaded"))
        hi_split, split_done, in_used = sem("hi_split"), sem("split_done"), sem("in_used")
        sq_done, rstd_done, hn_done, norm_tr, hT_hi_done, hT_lo_done = (sem(n) for n in (
            "sq_done", "rstd_done", "hn_done", "norm_tr", "hT_hi_done", "hT_lo_done"))
        proj_done, p_act, p_dve = sem("proj_done"), sem("p_act"), sem("p_dve")
        rope_step = sem("rope_step")
        q_zeroed, ta_tr, ta_act, ta_dve = sem("q_zeroed"), sem("ta_tr"), sem("ta_act"), sem("ta_dve")
        vb_fill = sem("vb_fill")
        tb_tr, tb_act, tb_dve, tb_fill = sem("tb_tr"), sem("tb_act"), sem("tb_dve"), sem("tb_fill")
        squared, tc_rs, tc_n = sem("squared"), sem("tc_rs"), sem("tc_n")
        sp_passed, pool_passed, pe_passed = sem("sp_passed"), sem("pool_passed"), sem("pe_passed")
        power_set, eps_added = sem("power_set"), sem("eps_added")
        tc_tr, tc_act, tc_dve = sem("tc_tr"), sem("tc_act"), sem("tc_dve")
        up_done, up_act, up_dve, asm_tr, asm_act, asm_dve = (sem(n) for n in (
            "up_done", "up_act", "up_dve", "asm_tr", "asm_act", "asm_dve"))
        z_done, w_done, t_done, te_act, te_dve, pv_done, o_done = (
            {g: sem(f"{n}_{g}") for g in "ABC"} for n in (
                "z_done", "w_done", "t_done", "te_act", "te_dve", "pv_done", "o_done"))
        a_step, l_done, d_done, top_done = sem("a_step"), sem("l_done"), sem("d_done"), sem("top_done")
        topc_done, es_done = sem("topc_done"), sem("es_done")
        gab_rs, gc_rs, gab_n, gc_n, oT_tr, oT_hi, oT_lo = (sem(n) for n in (
            "gab_rs", "gc_rs", "gab_n", "gc_n", "oT_tr", "oT_hi", "oT_lo"))
        wo_done, wadd_done = sem("wo_done"), sem("wadd_done")
        mu_done, relu_done, msq_done, mhi_done, mlo_done, md_done, madd_done = (sem(n) for n in (
            "mu_done", "relu_done", "msq_done", "mhi_done", "mlo_done", "md_done", "madd_done"))
        dve_chain, stored = sem("dve_chain"), [sem("stored0"), sem("stored1")]

        units = {"A": [(h, b) for b in range(NT) for h in range(A_HEADS)],
                 "B": [(None, t) for t in range(NT)],
                 "C": [(h, b) for b in range(NT) for h in range(C_HEADS)]}
        NU = {g: len(u) for g, u in units.items()}

        def key_tiles(g, u):
            return B_HEADS if g == "B" else units[g][u][1] + 1

        def nth(g, u, odd):
            return (u + 1) // 2 if odd else u // 2 + 1

        def wait_moved(eng, g, L, u):
            half = NU[g] // 2
            if u % 2 == 0:
                eng.wait_ge(te_act[g], L * half + nth(g, u, False))
            else:
                eng.wait_ge(te_dve[g], L * half + nth(g, u, True))

        def b_cols(h):
            return (h % 2) * HALF + (h // 2) * P

        slot_of = [u % 4 for u in range(U_IN)] + list(range(U_OUT))
        mlp_order = [(kind, c, f) for kind, c in (("up", 0), ("down", 0), ("up", 1)) for f in range(2)]
        for c in range(1, NC):
            if c + 1 < NC:
                mlp_order += [("up", c + 1, 0), ("up", c + 1, 1)]
            mlp_order += [("down", c, 0), ("down", c, 1)]
        slot_of += [(c % 2) * 4 + (0 if kind == "up" else 2) + f for kind, c, f in mlp_order]

        def W(slot, lo=False):
            return (ws_lo if lo else ws_hi)[slot // 4][:, slot % 4, :]

        SQ_LATENT, SQ_A, SQ_B, SQ_ALL = 2 * NT, 3 * NT, 4 * NT, 5 * NT
        GROUPS = ((QA, 256, 0), (QB, 512, 256), (OC, 256, 768))

        def aT(part, group):
            parity, g = (group // 4) % 2, group % 4
            return part[:, 2 * parity + g % 2, (g // 2) * HALF:(g // 2 + 1) * HALF]

        with nc.Block() as block:

            @block.sync
            def _(sp_engine):
                sp = Waiter(sp_engine, "sp", apart=sp_passed)
                for dst, src in ((ident[:, :], ident_in), (masks_in[:, 0, :], causal_in), (masks_in[:, 1, :], chunk_in),
                                 (rope_c[:, :, :, :], rope_c_in)):
                    sp_engine.dma_start(dst, src).then_inc(consts_in, 16)
                def land(u, L, src, width=1024, split=1):
                    if u >= 2:
                        sp.wait_ge(split_done, L * U_ALL + u - 1)
                    dst = raw[:, u % 2, 0:width]
                    if split > 1:
                        dst = dst.rearrange("p (k n) -> p k n", k=split)
                    sp_engine.dma_start(dst, src).then_inc(raw_loaded[u % 2], 16)

                def layer(L_reg, L):
                    w_in_l = w_in[bass.ds(L_reg, 1), :, :].rearrange("a (k p) n -> p (a k) n", p=P)
                    w_out_l = w_out[bass.ds(L_reg, 1), :, :].rearrange("a (k p) n -> p (a k) n", p=P)
                    w1_l = w_mlp_in[bass.ds(L_reg, 1), :, :].rearrange("a (k p) n -> p (a k) n", p=P)

                    def w2(f):
                        return w_mlp_out[bass.ds(L_reg, 1), bass.ds(f * P, P), :].rearrange("a p n -> p (a n)")

                    def w1(f):
                        return w1_l[:, :, bass.ds(f * P, P)]

                    def load_gain(src, at, width):
                        sp_engine.dma_start(gain[:, at:at + width], src[bass.ds(L_reg, 1), :].rearrange("a n -> (a n)")
                                     .partition_broadcast(P)).then_inc(gain_loaded, 16)

                    load_gain(attn_norm, 0, D)
                    for a in range(2):
                        sp_engine.dma_start(sink[:, 4 * a:4 * a + 4],
                                     sink_logits[bass.ds(L_reg, 1), bass.ds(a, 4, 2)].rearrange("a h -> (a h)")
                                     .partition_broadcast(P),
                                     allow_slow_non_contiguous=True).then_inc(sink_loaded, 16)
                    for u in range(U_IN):
                        j, i = u // 4, u % 4
                        width = BLOCKS[j]
                        land(u, L, w_in_l[:, 2 * i:2 * i + 2, j * HALF:j * HALF + width], 2 * width, 2)
                    sp.wait_ge(hn_done, (2 * L + 1) * NT)
                    load_gain(mla_q_norm, 0, Q_RANK)
                    load_gain(mla_kv_norm, Q_RANK, KV_RANK)
                    for u in (16, 17, 18, 19):
                        land(u, L, w_out_l[:, 2 * (u - 16):2 * (u - 16) + 2, 0:HALF], 1024, 2)
                    sp.wait_ge(proj_done, (L + 1) * 4 * NT)
                    sp_engine.dma_start(rope_b[:], rope_b_in).then_inc(tab_loaded, 16)
                    for u in (20, 21):
                        i, j = (u - 16) % 4, (u - 16) // 4
                        land(u, L, w_out_l[:, 2 * i:2 * i + 2, j * HALF:(j + 1) * HALF], 1024, 2)
                    sp.wait_ge(w_done["A"], (L + 1) * NU["A"])
                    for k in range(2):
                        sp_engine.dma_start(w_uq[k][:, :], w_mla_uq[bass.ds(L_reg, 1), k * P:(k + 1) * P, :]
                                     .rearrange("a p n -> p (a n)")).then_inc(up_loaded, 16)
                    sp_engine.dma_start(w_ukv[:, :], w_mla_ukv[bass.ds(L_reg, 1), :, :]
                                 .rearrange("a p n -> p (a n)")).then_inc(up_loaded, 16)
                    sp.wait_ge(tc_n, (L + 1) * 2 * NT)
                    sp.wait_ge(up_done, (L + 1) * 2 * NT)
                    load_gain(group_norm, 0, D)
                    for u in (22, 23):
                        i, j = (u - 16) % 4, (u - 16) // 4
                        land(u, L, w_out_l[:, 2 * i:2 * i + 2, j * HALF:(j + 1) * HALF], 1024, 2)
                    sp.wait_ge(gab_n, (L + 1) * 2 * NT)
                    sp.wait_ge(gc_n, (L + 1) * NT)
                    load_gain(mlp_norm, 0, D)

                    v = U_M

                    def land_w1(v, f):
                        land(v, L, w1(f), 1024, NK)

                    for kind, c, f in mlp_order[:6]:
                        if kind == "up":
                            land_w1(v, 2 * c + f)
                        else:
                            land(v, L, w2(2 * c + f))
                        v += 1
                    with sp_engine.Fori(0, NC // 2 - 1) as i_reg:
                        i = Count(0, [(i_reg, 1)])
                        for k in range(2):
                            for n in range(4):
                                first = U_M + 6 + 4 * k + n
                                sp.wait_ge(split_done, L * U_ALL + 8 * i + (first - 1))
                                if n < 2:
                                    sp_engine.dma_start(raw[:, first % 2, :].rearrange("p (k n) -> p k n", k=NK),
                                                 w1(4 * i_reg + (4 + 2 * k + n))).then_inc(raw_loaded[first % 2], 16)
                                else:
                                    sp_engine.dma_start(raw[:, first % 2, :],
                                                 w2(4 * i_reg + (2 + 2 * k + n - 2))).then_inc(raw_loaded[first % 2], 16)
                    for f in range(2):
                        land(U_ALL - 2 + f, L, w2(NF - 2 + f))
                    sp.wait_ge(split_done, (L + 1) * U_ALL)
                    sp.wait_ge(msq_done, (L + 1) * 4 * NC)

                with sp_engine.Fori(0, depth) as L:
                    layer(L, Count(0, [(L, 1)]))
                sp_engine.dma_start(gain[:, 0:D], final_norm.partition_broadcast(P)).then_inc(gain_loaded, 16)
                for t in range(NT):
                    sp.wait_ge(hn_done, 2 * depth * NT + t + 1)
                    sp_engine.dma_start(out[0, t * P:(t + 1) * P, :], x[:, t, :]).then_inc(stored[t % 2], 16)
                for b in range(2):
                    sp.wait_ge(stored[b], 8 * NT)

            @block.gpsimd
            def _(pool_engine):
                pool = Waiter(pool_engine, "pool", apart=pool_passed)
                def unit(L, u, width=1024, used=None):
                    slot = slot_of[u]
                    if used is not None:
                        pool.wait_ge(*used)
                    pool.wait_ge(raw_loaded[u % 2], L * (8 * U_ALL) + 16 * (u // 2 + 1))
                    nc.gpsimd.tensor_copy(W(slot)[:, 0:width], raw[:, u % 2, 0:width]).then_inc(hi_split, 1)
                    pool.wait_ge(hi_split, L * U_ALL + u + 1)
                    nc.gpsimd.tensor_tensor(W(slot, True)[:, 0:width], raw[:, u % 2, 0:width],
                                            W(slot)[:, 0:width].bitcast(F32), ALU.subtract).then_inc(split_done, 1)

                added = [0]

                def root(L, mean, r, count_done):
                    nc.gpsimd.tensor_scalar(r, mean, EPS, 1.0, ALU.add, ALU.mult).then_inc(eps_added, 1)
                    added[0] += 1
                    pool.wait_ge(eps_added, L * ROOTS + added[0])
                    exponent = power[:, :, :].to_broadcast([P, 2, NT]) if len(r.shape) == 3 else power[:, 0, 0:1]
                    nc.gpsimd.tensor_tensor(r, r, exponent, ALU.pow).then_inc(count_done, 1)

                ROOTS = 2 * NT + 2 + NT

                def norm_roots(L, L2, first=0, last=NT):
                    for t in range(first, last):
                        pool.wait_ge(sq_done, L2 * NT + t + 1)
                        root(L, ms[:, t:t + 1], rs[:, t:t + 1], rstd_done)

                def projected(L, u):
                    j, i = u // 4, u % 4
                    return (in_used, L * 12 + 3 * j + i + 1) if i < 3 else (proj_done, L * 4 * NT + NT * (j + 1))

                def layer(L_reg, L):
                    added[0] = 0
                    for u in range(U_IN):
                        if u == 3:
                            norm_roots(L, 2 * L, 0, 2)
                        if u == 4:
                            norm_roots(L, 2 * L, 2, NT)
                        unit(L, u, 2 * BLOCKS[u // 4], projected(L, u - 4) if u >= 4 else None)
                    for u in range(16, 20):
                        if u == 19:
                            pool.wait_ge(proj_done, (L + 1) * 4 * NT)
                            for pr in range(2):
                                nc.gpsimd.memset(qT_A[pr][:, :, :], 0.0).then_inc(q_zeroed, 1)
                        unit(L, u, 1024, projected(L, u - 4))
                    pool.wait_ge(p_act, (L + 1) * 2 * NT)
                    pool.wait_ge(p_dve, (L + 1) * 2 * NT)
                    pool.wait_ge(tab_loaded, (L + 1) * 16)
                    n = 0
                    for t in range(NT):
                        for v, half, cos, sin, m2 in (
                            (p[:, t, QB:VB].rearrange("p (h d) -> p h d", d=HD), HD // 2,
                             rope_b[:, t, 0:1, :], rope_b[:, t, 1:2, :], turned[:, :, :]),
                            (p[:, t, KR:IN_W].rearrange("p (h d) -> p h d", d=ROPE_C), ROPE_C // 2,
                             rope_c[:, t, 0:1, :], rope_c[:, t, 1:2, :], turned[:, 0:1, 0:ROPE_C])):
                            heads, width = v.shape[1], 2 * half
                            for a in range(2):
                                nc.gpsimd.tensor_tensor(
                                    m2[:, :, a * half:(a + 1) * half], v[:, :, (1 - a) * half:(2 - a) * half],
                                    sin[:, :, a * half:(a + 1) * half].to_broadcast([P, heads, half]),
                                    ALU.mult).then_inc(rope_step, 1)
                            n += 2
                            pool.wait_ge(rope_step, L * (2 * 4 * NT) + n)
                            nc.gpsimd.tensor_tensor(v, v, cos.to_broadcast([P, heads, width]),
                                                    ALU.mult).then_inc(rope_step, 1)
                            n += 1
                            pool.wait_ge(rope_step, L * (2 * 4 * NT) + n)
                            nc.gpsimd.tensor_tensor(v, v, m2, ALU.add).then_inc(rope_step, 1)
                            n += 1
                            pool.wait_ge(rope_step, L * (2 * 4 * NT) + n)
                    pool.wait_ge(z_done["A"], (L + 1) * NU["A"])
                    nc.gpsimd.memset(v_Bs[0:HD, 0, :], 0.0).then_inc(vb_fill, 1)
                    pool.wait_ge(vb_fill, L * 3 + 1)
                    nc.gpsimd.tensor_copy(v_Bs[0:HD, 1:NT, :], p[HD:P, 0:NT - 1, VB:VB + P]).then_inc(vb_fill, 1)
                    pool.wait_ge(vb_fill, L * 3 + 2)
                    nc.gpsimd.tensor_copy(v_Bs[HD:P, :, :], p[0:HD, :, VB:VB + P]).then_inc(vb_fill, 1)
                    pool.wait_ge(vb_fill, L * 3 + 3)
                    pool.wait_ge(squared, L * SQ_ALL + SQ_LATENT)
                    root(L, gms[:, 0:2, :], grs[:, 0:2, :], tc_rs)
                    pool.wait_ge(squared, L * SQ_ALL + SQ_B)
                    root(L, gms[:, 2:4, :], grs[:, 2:4, :], gab_rs)
                    for t in range(NT):
                        pool.wait_ge(squared, L * SQ_ALL + SQ_B + t + 1)
                        root(L, gms[:, 4, t:t + 1], grs[:, 4, t:t + 1], gc_rs)
                    for u in range(20, 24):
                        row_end = (16 * KB_ + (u - 20 + 1) * 4 * KB_ - 1) // (4 * IN_W)
                        pool.wait_ge(oT_tr, L * 2 * NT + 2 * (row_end + 1))
                        unit(L, u)
                    for v in range(6):
                        if v < 4:
                            norm_roots(L, 2 * L + 1, v, v + 1)
                        elif v == 4:
                            norm_roots(L, 2 * L + 1, v, NT)
                        unit(L, U_M + v, 1024,
                             (wo_done, L * 2 * NT + NT * (1 if slot_of[U_M + v] < 4 else 2)))
                    G, M = L * 4 * NC, L * 16 * NC
                    with pool_engine.Fori(0, NC // 2 - 1) as i_reg:
                        i = Count(0, [(i_reg, 1)])
                        for m in range(8):
                            first = U_M + 6 + m
                            s, s2 = slot_of[first], first % 2
                            if m % 4 < 2:
                                pool.wait_ge(mu_done, G + 8 * i + (m + 3))
                            else:
                                pool.wait_ge(md_done, M + 32 * i + (16 * (m // 4) or 1))
                            pool.wait_ge(raw_loaded[s2], L * (8 * U_ALL) + 64 * i + 16 * (first // 2 + 1))
                            nc.gpsimd.tensor_copy(W(s), raw[:, s2, :]).then_inc(hi_split, 1)
                            pool.wait_ge(hi_split, L * U_ALL + 8 * i + (first + 1))
                            nc.gpsimd.tensor_tensor(W(s, True), raw[:, s2, :], W(s).bitcast(F32),
                                                    ALU.subtract).then_inc(split_done, 1)
                    for f in range(2):
                        unit(L, U_ALL - 2 + f, 1024, (md_done, M + 16 * (NC - 2)))
                    pool.wait_ge(md_done, M + 16 * (NC - 1))
                    assert added[0] == ROOTS

                nc.gpsimd.memset(power[:, :, :], -0.5).then_inc(power_set, 1)
                pool.wait_ge(power_set, 1)
                with pool_engine.Fori(0, depth) as L:
                    layer(L, Count(0, [(L, 1)]))
                added[0] = 0
                norm_roots(depth, 2 * depth)

            @block.scalar
            def _(act_engine):
                act = Waiter(act_engine, "act")
                for t in range(NT):
                    if t == 2:
                        act.wait_ge(raw_loaded[1], 16)
                    if t == 4:
                        act.wait_ge(raw_loaded[0], 32)
                    act_engine.dma_start(x[:, t, :], x_in[0, t * P:(t + 1) * P, :]).then_inc(x_loaded[t], 16)
                nc.scalar.preload_act_table_set("natural_log_exp_and_others")
                def norm_row(L2, t, x_ready):
                    x_ready()
                    if t >= 2:
                        act.wait_ge(norm_tr, L2 * 2 * NT + 2 * (t - 1))
                    nc.scalar.activation(hn[:, t % 2, :], x[:, t, :], ACT.Square, scale=D ** -0.5,
                                         accum_out=ms[:, t:t + 1]).then_inc(sq_done, 1)

                def hT_high(L2, t):
                    for j in range(2):
                        q = 2 * t + j
                        act.wait_ge(norm_tr, L2 * 2 * NT + q + 1)
                        nc.scalar.activation(hT_hi[:, 4 * j:4 * j + 4, t * P:(t + 1) * P],
                                             B(4 + q % 4).rearrange("p (k n) -> p k n", k=4),
                                             ACT.Copy).then_inc(hT_hi_done, 1)

                def norm(L2, x_ready):
                    for t in range(NT):
                        norm_row(L2, t, lambda t=t: x_ready(t))
                        if t >= 1:
                            hT_high(L2, t - 1)
                    hT_high(L2, NT - 1)

                def move_T(g, L, u):
                    act.wait_ge(t_done[g], L * NU[g] + u + 1)
                    n = key_tiles(g, u) * P
                    nc.scalar.activation(wT[:, u % 2, 0:n], pair(2)[:, 0:n], ACT.Copy).then_inc(te_act[g], 1)

                summed = [0]

                def square(L, row, t, at, width):
                    n = summed[0]
                    summed[0] += 1
                    if n >= 2:
                        act.wait_ge(squared, L * SQ_ALL + n - 1)
                    nc.scalar.activation(squares[:, n % 2, 0:width], p[:, t, at:at + width], ACT.Square,
                                         scale=width ** -0.5, accum_out=gms[:, row, t:t + 1]).then_inc(squared, 1)

                def layer(L_reg, L):
                    summed[0] = 0
                    def x_ready(t):
                        act.wait_ge(x_loaded[t], 16)
                        act.wait_ge(madd_done, L * 16 * NC + (2 * t + 2))
                    norm(2 * L, x_ready)

                    for j in range(4):
                        for t in range(0, NT, 2):
                            act.wait_ge(proj_done, L * 4 * NT + NT * j + t + 1)
                            nc.scalar.activation(p[:, t, j * HALF:j * HALF + BLOCKS[j]], B(t)[:, 0:BLOCKS[j]],
                                                 ACT.Copy).then_inc(p_act, 1)

                    for i in range(0, 8, 2):
                        act.wait_ge(ta_tr, L * 8 + i + 1)
                        if i < 4:
                            act.wait_ge(q_zeroed, L * 2 + i // 2 + 1)
                            for e in range(2):
                                rows = slice(e * HD, (e + 1) * HD)
                                nc.scalar.activation(qT_A[i // 2][rows, e, 0:HALF], B(i)[rows, :], ACT.Copy,
                                                     scale=SCALE_A).then_inc(ta_act, 1)
                        else:
                            nc.scalar.activation(kT_A[:, i // 2 - 2, 0:HALF], B(i), ACT.Copy).then_inc(ta_act, 1)

                    def softplus_part(u):
                        n = key_tiles("A", u) * P
                        e = e_buf[:, u % 2, 0:n]
                        act.wait_ge(z_done["A"], L * NU["A"] + u + 1)
                        nc.scalar.activation(e, pair(u % 2)[:, 0:n], ACT.Abs).then_inc(a_step, 1)
                        act.wait_ge(a_step, L * 2 * NU["A"] + 2 * u + 1)
                        nc.scalar.activation(e, e, ACT.Exp, scale=-1.0).then_inc(a_step, 1)
                        act.wait_ge(a_step, L * 2 * NU["A"] + 2 * u + 2)
                        nc.scalar.activation(e, e, ACT.Ln, bias=1.0).then_inc(l_done, 1)

                    def stick_weights(u):
                        n = key_tiles("A", u) * P
                        act.wait_ge(d_done, L * NU["A"] + u + 1)
                        if u >= 2:
                            act.wait_ge(t_done["A"], L * NU["A"] + u - 1)
                        nc.scalar.activation(w_buf[:, u % 2, 0:n], c_buf[:, u % 2, 0:n],
                                             ACT.Exp).then_inc(w_done["A"], 1)

                    softplus_part(0)
                    for u in range(NU["A"] + 2):
                        if u >= 2 and u % 2 == 0:
                            move_T("A", L, u - 2)
                        if 1 <= u <= NU["A"]:
                            stick_weights(u - 1)
                        if u + 1 < NU["A"]:
                            softplus_part(u + 1)

                    for i in range(2):
                        act.wait_ge(tb_tr, L * 10 + i + 1)
                        at = HD + i * HALF
                        nc.scalar.activation(kT_B[:, at:at + HALF], B(i), ACT.Copy).then_inc(tb_act, 1)
                    for i in range(2, 10, 2):
                        act.wait_ge(tb_tr, L * 10 + i + 1)
                        nc.scalar.activation(qT_B[:, i // 2 - 1, 0:HALF], B(i % 8), ACT.Copy,
                                             scale=SCALE_A).then_inc(tb_act, 1)

                    def window_weights(u):
                        act.wait_ge(top_done, L * NT + u + 1)
                        if u >= 2:
                            act.wait_ge(t_done["B"], L * NU["B"] + u - 1)
                        nc.scalar.activation(psm[:, u, :], top[:, u % 2, :], ACT.Exp).then_inc(es_done, 1)
                        for m in range(B_HEADS):
                            last = nc.scalar.activation(w_buf[:, u % 2, m * P:(m + 1) * P],
                                                        pair(u % 2)[:, m * P:(m + 1) * P], ACT.Exp,
                                                        bias=ntop[:, u % 2, m:m + 1],
                                                        accum_out=rden[:, u, m:m + 1])
                        last.then_inc(w_done["B"], 1)

                    for u in range(NU["B"] + 2):
                        if u >= 2 and u % 2 == 0:
                            move_T("B", L, u - 2)
                        if u < NU["B"]:
                            window_weights(u)
                            if u < 4:
                                for t in (2 * u, 2 * u + 1):
                                    square(L, 0, t, CQ, Q_RANK)
                                    square(L, 1, t, CKV, KV_RANK)
                            else:
                                if u == 4:
                                    act.wait_ge(o_done["A"], (L + 1) * NU["A"])
                                for t in (2 * u - 8, 2 * u - 7):
                                    square(L, 2, t, *GROUPS[0][:2])

                    act.wait_ge(squared, L * SQ_ALL + SQ_A)
                    for i in range(0, 6, 2):
                        act.wait_ge(tc_tr, L * 6 + i + 1)
                        dst = (cqT[:, i // 2, 0:HALF] if i < 4 else ckvT[:, 0:HALF])
                        nc.scalar.activation(dst, B(i), ACT.Copy).then_inc(tc_act, 1)
                    for t in range(NT + 1):
                        if t < NT:
                            b0 = 2 * (t % 2)
                            act.wait_ge(up_done, L * 2 * NT + 2 * t + 1)
                            if t >= 2:
                                act.wait_ge(asm_tr, L * 2 * NT + 2 * (t - 1))
                            nc.scalar.activation(
                                qk_asm[:, t % 2, 0, :, 0:HD],
                                B(b0)[:, 0:C_HEADS * QK_C].rearrange("p (h d) -> p h d", d=QK_C)[:, :, 0:HD],
                                ACT.Copy).then_inc(up_act, 1)
                            act.wait_ge(up_done, L * 2 * NT + 2 * t + 2)
                            kv = B(b0 + 1).rearrange("p (h d) -> p h d", d=2 * HD)
                            nc.scalar.activation(qk_asm[:, t % 2, 1, :, 0:HD], kv[:, :, 0:HD],
                                                 ACT.Copy).then_inc(up_act, 1)
                            nc.scalar.activation(p[:, t, VA:VA + C_HEADS * HD].rearrange("p (h d) -> p h d", d=HD),
                                                 kv[:, :, HD:2 * HD], ACT.Copy).then_inc(up_act, 1)
                        if t >= 1:
                            act.wait_ge(asm_tr, L * 2 * NT + 2 * (t - 1) + 1)
                            nc.scalar.activation(qT_C[0:QK_C, :, (t - 1) * P:t * P],
                                                 B(4)[0:QK_C, :].rearrange("p (h n) -> p h n", h=C_HEADS),
                                                 ACT.Copy).then_inc(asm_act, 1)

                    def latent_weights(u):
                        h, b = units["C"][u]
                        n = (b + 1) * P
                        act.wait_ge(topc_done, L * NU["C"] + u + 1)
                        if u >= 2:
                            act.wait_ge(t_done["C"], L * NU["C"] + u - 1)
                        nc.scalar.activation(w_buf[:, u % 2, 0:n], pair(u % 2)[:, 0:n], ACT.Exp,
                                             bias=ntop[:, u % 2, 0:1], scale=SCALE_C,
                                             accum_out=psm[:, b, h:h + 1]).then_inc(w_done["C"], 1)

                    for u in range(NU["C"] + 2):
                        if u >= 2 and u % 2 == 0:
                            move_T("C", L, u - 2)
                        if u < NU["C"]:
                            latent_weights(u)
                        if u < NT:
                            if u == 0:
                                act.wait_ge(o_done["B"], (L + 1) * NU["B"])
                            square(L, 3, u, *GROUPS[1][:2])
                        if u >= 7 and u % 4 == 3:
                            act.wait_ge(o_done["C"], L * NU["C"] + u - 3)
                            square(L, 4, (u - 7) // 4, *GROUPS[2][:2])
                    act.wait_ge(o_done["C"], (L + 1) * NU["C"])
                    square(L, 4, NT - 1, *GROUPS[2][:2])
                    act.wait_ge(squared, (L + 1) * SQ_ALL)
                    for q in range(2 * NT):
                        t, j = q // 2, q % 2
                        act.wait_ge(oT_tr, L * 2 * NT + q + 1)
                        nc.scalar.activation(hT_hi[:, 4 * j:4 * j + 4, t * P:(t + 1) * P],
                                             B(4 + q % 4).rearrange("p (k n) -> p k n", k=4),
                                             ACT.Copy).then_inc(oT_hi, 1)

                    norm(2 * L + 1, lambda t: act.wait_ge(wadd_done, L * 2 * NT + NT + t + 1))

                    def relu(G0, first):
                        act.wait_ge(mu_done, G0 + (first + 1))
                        if first >= 2:
                            act.wait_ge(msq_done, G0 + (first - 1))
                        nc.scalar.activation(relu_t[:, first % 2, :], B(first % 4), ACT.Relu).then_inc(relu_done, 1)

                    def high(G0, first):
                        act.wait_ge(msq_done, G0 + (first + 1))
                        nc.scalar.activation(aT(aT_hi, first), B(first % 4),
                                             ACT.Copy).then_inc(mhi_done, 1)

                    def groups(G0, first):
                        for g in range(4):
                            relu(G0, first + g)
                            if g >= 1:
                                high(G0, first + g - 1)
                        high(G0, first + 3)

                    groups(L * 4 * NC, 0)
                    groups(L * 4 * NC, 4)
                    with act_engine.Fori(0, NC // 2 - 1) as i_reg:
                        i = Count(0, [(i_reg, 1)])
                        groups(L * 4 * NC + 8 * i, 8)
                        groups(L * 4 * NC + 8 * i, 12)

                with act_engine.Fori(0, depth) as L:
                    layer(L, Count(0, [(L, 1)]))

                for t in range(NT):
                    act.wait_ge(madd_done, depth * 16 * NC + 2 * t + 2)
                    if t >= 2:
                        act.wait_ge(sq_done, 2 * depth * NT + t - 1)
                    nc.scalar.activation(hn[:, t % 2, :], x[:, t, :], ACT.Square, scale=D ** -0.5,
                                         accum_out=ms[:, t:t + 1]).then_inc(sq_done, 1)

            @block.vector
            def _(dve_engine):
                dve = Waiter(dve_engine, "dve")
                chain = [0]
                DVE_LINKS = 2 * NU["A"] + 2 + 4 * NT + 2 * NU["C"]


                def link(ins, L):
                    chain[0] += 1
                    ins.then_inc(dve_chain, 1)
                    dve.wait_ge(dve_chain, L * DVE_LINKS + chain[0])

                def norm_row(L2, t, gains, into=None):
                    dve.wait_ge(rstd_done, L2 * NT + t + 1)
                    if t == 0:
                        dve.wait_ge(gain_loaded, gains)
                    nc.vector.scalar_tensor_tensor(hn[:, t % 2, :] if into is None else into, x[:, t, :], rs[:, t:t + 1], gain[:, 0:D],
                                                   ALU.mult, ALU.mult).then_inc(hn_done, 1)

                def hT_low(L2, t):
                    for j in range(2):
                        q = 2 * t + j
                        dve.wait_ge(hT_hi_done, L2 * 2 * NT + q + 1)
                        dst = slice(t * P, (t + 1) * P)
                        nc.vector.tensor_tensor(hT_lo[:, 4 * j:4 * j + 4, dst],
                                                B(4 + q % 4).rearrange("p (k n) -> p k n", k=4),
                                                hT_hi[:, 4 * j:4 * j + 4, dst].bitcast(F32),
                                                ALU.subtract).then_inc(hT_lo_done, 1)

                def move_T(g, L, u):
                    dve.wait_ge(t_done[g], L * NU[g] + u + 1)
                    n = key_tiles(g, u) * P
                    nc.vector.tensor_copy(wT[:, u % 2, 0:n], pair(2)[:, 0:n]).then_inc(te_dve[g], 1)

                def layer(L_reg, L):
                    chain[0] = 0
                    for t in range(NT):
                        norm_row(2 * L, t, L * 80 + 16)
                        if t >= 1:
                            hT_low(2 * L, t - 1)
                    hT_low(2 * L, NT - 1)

                    for j in range(4):
                        for t in range(1, NT, 2):
                            dve.wait_ge(proj_done, L * 4 * NT + NT * j + t + 1)
                            nc.vector.tensor_copy(p[:, t, j * HALF:j * HALF + BLOCKS[j]],
                                                  B(t)[:, 0:BLOCKS[j]]).then_inc(p_dve, 1)

                    for i in range(1, 8, 2):
                        dve.wait_ge(ta_tr, L * 8 + i + 1)
                        if i < 4:
                            dve.wait_ge(q_zeroed, L * 2 + i // 2 + 1)
                            for e in range(2):
                                rows = slice(e * HD, (e + 1) * HD)
                                nc.vector.tensor_scalar(qT_A[i // 2][rows, e, HALF:S], B(i)[rows, :], SCALE_A, None,
                                                        ALU.mult).then_inc(ta_dve, 1)
                        else:
                            nc.vector.tensor_copy(kT_A[:, i // 2 - 2, HALF:S], B(i)).then_inc(ta_dve, 1)

                    def stick_sums(u):
                        n = key_tiles("A", u) * P
                        z, e, c = pair(u % 2)[:, 0:n], e_buf[:, u % 2, 0:n], c_buf[:, u % 2, 0:n]
                        dve.wait_ge(l_done, L * NU["A"] + u + 1)
                        if u >= 2:
                            dve.wait_ge(w_done["A"], L * NU["A"] + u - 1)
                        link(nc.vector.scalar_tensor_tensor(c, z, 0.0, e, ALU.max, ALU.add), L)
                        link(nc.vector.tensor_tensor_scan(e[:, ::-1], c[:, ::-1], c[:, ::-1], 0.0,
                                                          ALU.add, ALU.bypass), L)
                        nc.vector.tensor_tensor(c, z, e, ALU.subtract).then_inc(d_done, 1)

                    def out_A(u):
                        h, b = units["A"][u]
                        dve.wait_ge(pv_done["A"], L * NU["A"] + u + 1)
                        nc.vector.tensor_copy(p[:, b, QA + h * HD:QA + (h + 1) * HD],
                                              B(6 + u % 2)[:, 0:HD]).then_inc(o_done["A"], 1)

                    def fill_B():
                        dve.wait_ge(rope_step, (L + 1) * 8 * NT)
                        nc.vector.memset(kT_B[:, 0:HD], 0.0).then_inc(tb_fill, 1)
                        nc.vector.memset(kT_Bs[:, 0:HD], 0.0).then_inc(tb_fill, 1)
                        dve.wait_ge(sink_loaded, L * 32 + 32)
                        link(nc.vector.tensor_scalar(nsink[:, :], sink[:, :], -1.0, None, ALU.mult), L)

                    for u in range(NU["A"] + 3):
                        if u == NU["A"] - 6:
                            fill_B()
                        if 2 <= u < NU["A"] + 2 and u % 2 == 1:
                            move_T("A", L, u - 2)
                        if u >= 3:
                            out_A(u - 3)
                        if u < NU["A"]:
                            stick_sums(u)

                    for i in range(2):
                        dve.wait_ge(tb_act, L * 6 + 1 + i)
                        at = HD + i * HALF
                        nc.vector.tensor_copy(kT_Bs[0:HD, at:at + HALF], B(i)[HD:P, :]).then_inc(tb_fill, 1)
                        nc.vector.tensor_copy(kT_Bs[HD:P, at:at + HALF], B(i)[0:HD, :]).then_inc(tb_fill, 1)
                    for i in range(3, 10, 2):
                        dve.wait_ge(tb_tr, L * 10 + i + 1)
                        nc.vector.tensor_scalar(qT_B[:, i // 2 - 1, HALF:S], B(i % 8), SCALE_A, None,
                                                ALU.mult).then_inc(tb_dve, 1)

                    def window_top(u):
                        s = pair(u % 2).rearrange("p (h n) -> p h n", h=B_HEADS)
                        dve.wait_ge(z_done["B"], L * NU["B"] + u + 1)
                        if u == 0:
                            link(nc.vector.memset(s[0:HD, :, 0:HD], BIG), L)
                        link(nc.vector.tensor_reduce(ntop[:, u % 2, :], s, AX_X, ALU.max, negate=True), L)
                        link(nc.vector.tensor_tensor(ntop[:, u % 2, :], ntop[:, u % 2, :], nsink[:, :], ALU.min), L)
                        if u >= 2:
                            dve.wait_ge(es_done, L * NT + u - 1)
                        nc.vector.tensor_tensor(top[:, u % 2, :], ntop[:, u % 2, :], sink[:, :],
                                                ALU.add).then_inc(top_done, 1)

                    def out_B(u):
                        dve.wait_ge(w_done["B"], L * NU["B"] + u + 1)
                        link(nc.vector.tensor_tensor(rden[:, u, :], rden[:, u, :], psm[:, u, :],
                                                     ALU.add), L)
                        link(nc.vector.reciprocal(rden[:, u, :], rden[:, u, :]), L)
                        dve.wait_ge(pv_done["B"], L * NU["B"] + u + 1)
                        r = rden[:, u, :].rearrange("p (e h) -> p h e", e=2).unsqueeze(3)
                        nc.vector.tensor_tensor(
                            p[:, u, QB:KB].rearrange("p (h e d) -> p h e d", e=2, d=HD),
                            B(6 + u % 2).rearrange("p (h e d) -> p h e d", e=2, d=HD),
                            r.to_broadcast([P, 4, 2, HD]), ALU.mult).then_inc(o_done["B"], 1)

                    def scale_rows(row, t, at, width, to):
                        v = p[:, t, at:at + width]
                        return nc.vector.scalar_tensor_tensor(v, v, grs[:, row, t:t + 1], gain[:, to:to + width],
                                                              ALU.mult, ALU.mult)

                    def normalise_latents(t):
                        scale_rows(0, t, CQ, Q_RANK, 0).then_inc(tc_n, 1)
                        scale_rows(1, t, CKV, KV_RANK, Q_RANK).then_inc(tc_n, 1)

                    window_top(0)
                    for u in range(NU["B"] + 3):
                        if 2 <= u < NU["B"] + 2 and u % 2 == 1:
                            move_T("B", L, u - 2)
                        if u >= 3:
                            out_B(u - 3)
                        if u + 1 < NU["B"]:
                            window_top(u + 1)
                        if u == 5:
                            dve.wait_ge(tc_rs, L + 1)
                            dve.wait_ge(gain_loaded, L * 80 + 48)
                        if 5 <= u < 9:
                            normalise_latents(2 * (u - 5))
                            normalise_latents(2 * (u - 5) + 1)

                    dve.wait_ge(squared, L * SQ_ALL + SQ_A)
                    for i in range(1, 6, 2):
                        dve.wait_ge(tc_tr, L * 6 + i + 1)
                        dst = (cqT[:, i // 2, HALF:S] if i < 4 else ckvT[:, HALF:S])
                        nc.vector.tensor_copy(dst, B(i)).then_inc(tc_dve, 1)
                    dve.wait_ge(rope_step, (L + 1) * 8 * NT)
                    for t in range(NT + 1):
                        if t < NT:
                            b0 = 2 * (t % 2)
                            if t >= 2:
                                dve.wait_ge(asm_tr, L * 2 * NT + 2 * (t - 1))
                            dve.wait_ge(up_act, L * 3 * NT + 3 * t + 3)
                            q = B(b0)[:, 0:C_HEADS * QK_C].rearrange("p (h d) -> p h d", d=QK_C)[:, :, HD:QK_C]
                            cos, sin = (rope_c[:, t, a:a + 1, :] for a in range(2))
                            m1, m2 = rope_t[:, t % 2, 0, :, :], rope_t[:, t % 2, 1, :, :]
                            hf = ROPE_C // 2
                            nc.vector.tensor_tensor(m1, q, cos.to_broadcast([P, C_HEADS, ROPE_C]),
                                                    ALU.mult).then_inc(up_dve, 1)
                            for a in range(2):
                                nc.vector.tensor_tensor(
                                    m2[:, :, a * hf:(a + 1) * hf], q[:, :, (1 - a) * hf:(2 - a) * hf],
                                    sin[:, :, a * hf:(a + 1) * hf].to_broadcast([P, C_HEADS, hf]),
                                    ALU.mult).then_inc(up_dve, 1)
                            dve.wait_ge(up_dve, L * 5 * NT + 5 * t + 3)
                            nc.vector.tensor_tensor(qk_asm[:, t % 2, 0, :, HD:QK_C], m1, m2,
                                                    ALU.add).then_inc(up_dve, 1)
                            nc.vector.tensor_copy(
                                qk_asm[:, t % 2, 1, :, HD:QK_C],
                                p[:, t, KR:IN_W].unsqueeze(1).to_broadcast([P, C_HEADS, ROPE_C])).then_inc(up_dve, 1)
                        if t >= 1:
                            dve.wait_ge(asm_tr, L * 2 * NT + 2 * (t - 1) + 2)
                            nc.vector.tensor_copy(kT_C[0:QK_C, :, (t - 1) * P:t * P],
                                                  B(5)[0:QK_C, :].rearrange("p (h n) -> p h n", h=C_HEADS)
                                                  ).then_inc(asm_dve, 1)

                    def latent_top(u):
                        n = key_tiles("C", u) * P
                        dve.wait_ge(z_done["C"], L * NU["C"] + u + 1)
                        link(nc.vector.tensor_reduce(top[:, u % 2, 0:1], pair(u % 2)[:, 0:n], AX_X, ALU.max), L)
                        nc.vector.tensor_scalar(ntop[:, u % 2, 0:1], top[:, u % 2, 0:1], -SCALE_C, None,
                                                ALU.mult).then_inc(topc_done, 1)

                    def out_C(u):
                        h, b = units["C"][u]
                        dve.wait_ge(w_done["C"], L * NU["C"] + u + 1)
                        link(nc.vector.reciprocal(rden[:, b, h:h + 1], psm[:, b, h:h + 1]), L)
                        dve.wait_ge(pv_done["C"], L * NU["C"] + u + 1)
                        nc.vector.tensor_scalar(p[:, b, OC + h * HD:OC + (h + 1) * HD], B(6 + u % 2)[:, 0:HD],
                                                rden[:, b, h:h + 1], None, ALU.mult).then_inc(o_done["C"], 1)

                    AB_FROM = 13

                    def normalise_C(t):
                        dve.wait_ge(gc_rs, L * NT + t + 1)
                        scale_rows(4, t, *GROUPS[2]).then_inc(gc_n, 1)

                    latent_top(0)
                    for u in range(NU["C"] + 3):
                        if 2 <= u < NU["C"] + 2 and u % 2 == 1:
                            move_T("C", L, u - 2)
                        if u >= 3:
                            out_C(u - 3)
                        if u + 1 < NU["C"]:
                            latent_top(u + 1)
                        if u == AB_FROM:
                            dve.wait_ge(gab_rs, L + 1)
                            dve.wait_ge(gain_loaded, L * 80 + 64)
                        if AB_FROM <= u < AB_FROM + 2 * NT:
                            g, t = (u - AB_FROM) // NT, (u - AB_FROM) % NT
                            scale_rows(2 + g, t, *GROUPS[g]).then_inc(gab_n, 1)
                        if u >= 14 and u % 4 == 2:
                            normalise_C((u - 14) // 4)
                    normalise_C(NT - 2)

                    oT_low(L, 0)
                    oT_low(L, 1)
                    normalise_C(NT - 1)
                    for m in range(2 * NT):
                        half, t = m // NT, m % NT
                        if 1 <= m < NT // 2:
                            oT_low(L, 2 * m)
                            oT_low(L, 2 * m + 1)
                        dve.wait_ge(wo_done, L * 2 * NT + m + 1)
                        xs = x[:, t, half * HALF:(half + 1) * HALF]
                        nc.vector.tensor_tensor(xs, B(m % 4), xs, ALU.add).then_inc(wadd_done, 1)
                        if half == 1:
                            dve.wait_ge(wadd_done, L * 2 * NT + m + 1)
                            norm_row(2 * L + 1, t, L * 80 + 80)
                            if t >= 1:
                                hT_low(2 * L + 1, t - 1)
                    hT_low(2 * L + 1, NT - 1)

                    def square(G0, first):
                        dve.wait_ge(relu_done, G0 + (first + 1))
                        nc.vector.scalar_tensor_tensor(B(first % 4), B(first % 4), 0.0, relu_t[:, first % 2, :],
                                                       ALU.max, ALU.mult).then_inc(msq_done, 1)

                    def low(G0, first):
                        dve.wait_ge(mhi_done, G0 + (first + 1))
                        nc.vector.tensor_tensor(aT(aT_lo, first), B(first % 4),
                                                aT(aT_hi, first).bitcast(F32),
                                                ALU.subtract).then_inc(mlo_done, 1)

                    def groups(G0, first):
                        for g in range(4):
                            square(G0, first + g)
                            if g >= 1:
                                low(G0, first + g - 1)
                        low(G0, first + 3)

                    def adds(M0, first):
                        for m in range(16):
                            t, half = m // 2, m % 2
                            dve.wait_ge(md_done, M0 + (first + m + 1))
                            dve.wait_ge(madd_done, M0 + (first + m + 1))
                            xs = x[:, t, half * HALF:(half + 1) * HALF]
                            nc.vector.tensor_tensor(xs, B(4 + m % 4), xs, ALU.add).then_inc(madd_done, 1)

                    G, M = L * 4 * NC, L * 16 * NC
                    groups(G, 0)
                    groups(G, 4)
                    adds(M, 0)
                    with dve_engine.Fori(0, NC // 2 - 1) as i_reg:
                        i = Count(0, [(i_reg, 1)])
                        groups(G + 8 * i, 8)
                        adds(M + 32 * i, 16)
                        groups(G + 8 * i, 12)
                        adds(M + 32 * i, 32)
                    adds(M, 16 * (NC - 1))
                    assert chain[0] == DVE_LINKS, chain[0]

                def oT_low(L, t):
                    for j in range(2):
                        q = 2 * t + j
                        dve.wait_ge(oT_hi, L * 2 * NT + q + 1)
                        dst = slice(t * P, (t + 1) * P)
                        nc.vector.tensor_tensor(hT_lo[:, 4 * j:4 * j + 4, dst],
                                                B(4 + q % 4).rearrange("p (k n) -> p k n", k=4),
                                                hT_hi[:, 4 * j:4 * j + 4, dst].bitcast(F32),
                                                ALU.subtract).then_inc(oT_lo, 1)

                dve.wait_ge(consts_in, 4 * 16)
                nc.vector.tensor_copy(identb[:, :], ident[:, :]).then_inc(masks_ready, 1)
                nc.vector.tensor_copy(causal[:, :], masks_in[:, 0, :]).then_inc(masks_ready, 1)
                nc.vector.tensor_copy(chunk[:, :], masks_in[:, 1, :]).then_inc(masks_ready, 1)
                dve_engine.sem_inc(madd_done, 16)
                with dve_engine.Fori(0, depth) as L:
                    layer(L, Count(0, [(L, 1)]))
                for t in range(NT):
                    norm_row(2 * depth, t, depth * 80 + 16, x[:, t, :])

            @block.tensor
            def _(pe_engine):
                pe = Waiter(pe_engine, "pe")
                mm = nc.tensor.matmul

                def three(out_, a, b, first, last):
                    mm(out_, a[0], b[0], start=first, stop=False)
                    mm(out_, a[0], b[1], start=False, stop=False)
                    return mm(out_, a[1], b[0], start=False, stop=last)

                def hT(k, cols):
                    return hT_hi[:, k, cols], hT_lo[:, k, cols]

                def turn_rows(done, src, q, k0):
                    for k in range(4):
                        last = nc.tensor.transpose(B(4 + q % 4)[:, k * P:(k + 1) * P], src(k0 + k), ident[:, :])
                    last.then_inc(done, 1)

                def norm_turn(L2, t):
                    pe.wait_ge(hn_done, L2 * NT + t + 1)
                    for j in range(2):
                        q = 2 * t + j
                        if q >= 4:
                            pe.wait_ge(hT_lo_done, L2 * 2 * NT + q - 3)
                        turn_rows(norm_tr, lambda k: hn[:, t % 2, k * P:(k + 1) * P], q, 4 * j)

                def layer(L_reg, L):
                    def project(j, i, t):
                        n, s = BLOCKS[j], slot_of[4 * j + i]
                        for kk in range(2):
                            k = 2 * i + kk
                            wcol = slice(kk * n, (kk + 1) * n)
                            last = three(B(t)[:, 0:n], hT(k, slice(t * P, (t + 1) * P)),
                                         (W(s)[:, wcol], W(s, True)[:, wcol]), k == 0, k == NK - 1)
                        if i == 3:
                            last.then_inc(proj_done, 1)
                        elif t == NT - 1:
                            last.then_inc(in_used, 1)

                    pe.wait_ge(madd_done, L * 16 * NC + 16)
                    for t in range(NT // 2):
                        norm_turn(2 * L, 2 * t)
                        norm_turn(2 * L, 2 * t + 1)
                        pe.wait_ge(hT_lo_done, 2 * L * 2 * NT + 2 * (t + 1))
                        for i in range(4):
                            if t == 0:
                                pe.wait_ge(split_done, L * U_ALL + i + 1)
                            project(0, i, t)
                    pe.wait_ge(hT_lo_done, 2 * L * 2 * NT + 2 * NT)
                    for i in range(4):
                        for t in range(NT // 2, NT):
                            project(0, i, t)
                    for j in range(1, 4):
                        for i in range(4):
                            pe.wait_ge(split_done, L * U_ALL + 4 * j + i + 1)
                            for t in range(NT):
                                if i == 0:
                                    pe.wait_ge(p_dve if t % 2 else p_act, L * 16 + 4 * (j - 1) + t // 2 + 1)
                                project(j, i, t)

                    pe.wait_ge(p_act, (L + 1) * 16)
                    pe.wait_ge(p_dve, (L + 1) * 16)
                    for i in range(8):
                        at = (QA if i < 4 else KA) + ((i // 2) % 2) * P
                        for tt in range(4):
                            t = 4 * (i % 2) + tt
                            last = nc.tensor.transpose(B(i)[:, tt * P:(tt + 1) * P], p[:, t, at:at + P], ident[:, :])
                        last.then_inc(ta_tr, 1)

                    def scores(g, u):
                        h, b = units[g][u]
                        z = pair(u % 2)
                        if g == "B":
                            for m in range(B_HEADS):
                                r = (m % 2) * HD
                                kT = kT_B if m % 2 == m // 4 else kT_Bs
                                for half in range(2):
                                    q0 = b * P + half * HD
                                    last = mm(z[half * HD:(half + 1) * HD, b_cols(m):b_cols(m) + P],
                                              qT_B[r:r + HD, m // 2, q0:q0 + HD], kT[r:r + HD, q0:q0 + P],
                                              start=True, stop=True)
                            last.then_inc(z_done[g], 1)
                            return
                        if g == "A":
                            q = qT_A[h // 2][:, h % 2, b * P:(b + 1) * P]
                            k = kT_A[:, h // 2, :]
                            mask = causal
                        else:
                            q = qT_C[0:QK_C, h, b * P:(b + 1) * P]
                            k = kT_C[0:QK_C, h, :]
                            mask = chunk
                        n = (b + 1) * P
                        for c0 in range(0, n, HALF):
                            c1 = min(n, c0 + HALF)
                            mm(z[:, c0:c1], q, k[:, c0:c1], start=True, stop=c1 < n)
                        mm(z[:, b * P:n], identb[:, :], mask[:, :], start=False, stop=True).then_inc(z_done[g], 1)

                    def turn_weights(g, L, u):
                        pe.wait_ge(w_done[g], L * NU[g] + u + 1)
                        if u >= 1:
                            wait_moved(pe, g, L, u - 1)
                        for kb in range(key_tiles(g, u)):
                            last = nc.tensor.transpose(pair(2)[:, kb * P:(kb + 1) * P],
                                                       w_buf[:, u % 2, kb * P:(kb + 1) * P], ident[:, :])
                        last.then_inc(t_done[g], 1)

                    def weigh_values(g, L, u):
                        if g == "B" and u == 0:
                            pe.wait_ge(vb_fill, (L + 1) * 3, apart=pe_passed)
                        wait_moved(pe, g, L, u)
                        if u >= 2:
                            pe.wait_ge(o_done[g], L * NU[g] + u - 1)
                        h, b = units[g][u]
                        o = B(6 + u % 2)
                        if g == "B":
                            for m in range(B_HEADS):
                                v0 = (m // 4) * HD
                                for half in range(2):
                                    v = (p[:, b, VB + v0:VB + v0 + HD] if half else v_Bs[:, b, v0:v0 + HD])
                                    c0 = b_cols(m) + half * HD
                                    last = mm(o[half * HD:(half + 1) * HD, m * HD:(m + 1) * HD],
                                              wT[:, u % 2, c0:c0 + HD], v, start=True, stop=True)
                        else:
                            for kb in range(b + 1):
                                last = mm(o[:, 0:HD], wT[:, u % 2, kb * P:(kb + 1) * P],
                                          p[:, kb, VA + h * HD:VA + (h + 1) * HD], start=kb == 0, stop=kb == b)
                        last.then_inc(pv_done[g], 1)

                    def attend(g, z_free):
                        passed = pe_passed if g == "B" else None
                        scores(g, 0)
                        for u in range(NU[g]):
                            if u + 1 < NU[g]:
                                if u >= 1:
                                    pe.wait_ge(z_free[0], L * NU[g] + u, apart=passed)
                                scores(g, u + 1)
                            if u >= 1:
                                turn_weights(g, L, u - 1)
                            if u >= 2:
                                weigh_values(g, L, u - 2)
                        turn_weights(g, L, NU[g] - 1)
                        weigh_values(g, L, NU[g] - 2)
                        weigh_values(g, L, NU[g] - 1)

                    pe.wait_ge(q_zeroed, (L + 1) * 2)
                    pe.wait_ge(ta_act, (L + 1) * 6)
                    pe.wait_ge(ta_dve, (L + 1) * 6)
                    attend("A", (d_done,))

                    pe.wait_ge(rope_step, (L + 1) * 8 * NT)
                    for i in range(10):
                        at = QB + (i // 2 - 1) * P if i >= 2 else KB
                        if i == 6:
                            pe.wait_ge(o_done["A"], (L + 1) * NU["A"])
                        if i >= 8:
                            pe.wait_ge(tb_act, L * 6 + i - 7)
                            pe.wait_ge(tb_fill, L * 6 + 2 + 2 * (i - 7))
                        for tt in range(4):
                            t = 4 * (i % 2) + tt
                            last = nc.tensor.transpose(B(i % 8)[:, tt * P:(tt + 1) * P], p[:, t, at:at + P],
                                                       ident[:, :])
                        last.then_inc(tb_tr, 1)
                    pe.wait_ge(tb_act, (L + 1) * 6)
                    pe.wait_ge(tb_dve, (L + 1) * 4)
                    pe.wait_ge(tb_fill, (L + 1) * 6, apart=pe_passed)
                    attend("B", (w_done["B"],))

                    pe.wait_ge(tc_n, (L + 1) * 2 * NT)
                    for i in range(6):
                        at = CQ + (i // 2) * P
                        for tt in range(4):
                            t = 4 * (i % 2) + tt
                            last = nc.tensor.transpose(B(i)[:, tt * P:(tt + 1) * P], p[:, t, at:at + P], ident[:, :])
                        last.then_inc(tc_tr, 1)
                    pe.wait_ge(tc_act, (L + 1) * 3)
                    pe.wait_ge(tc_dve, (L + 1) * 3)
                    pe.wait_ge(up_loaded, (L + 1) * 48)
                    for t in range(NT + 1):
                        if t < NT:
                            b0 = 2 * (t % 2)
                            tok = slice(t * P, (t + 1) * P)
                            if t >= 2:
                                pe.wait_ge(up_act, L * 3 * NT + 3 * (t - 1))
                                pe.wait_ge(up_dve, L * 5 * NT + 5 * (t - 2) + 3)
                            for k in range(2):
                                last = mm(B(b0)[:, 0:C_HEADS * QK_C], cqT[:, k, tok], w_uq[k][:, :],
                                          start=k == 0, stop=k == 1)
                            last.then_inc(up_done, 1)
                            mm(B(b0 + 1), ckvT[:, tok], w_ukv[:, :], start=True, stop=True).then_inc(up_done, 1)
                        if t >= 1:
                            s = (t - 1) % 2
                            pe.wait_ge(up_act, L * 3 * NT + 3 * t)
                            pe.wait_ge(up_dve, L * 5 * NT + 5 * t)
                            if t >= 2:
                                pe.wait_ge(asm_act, L * NT + t - 1)
                                pe.wait_ge(asm_dve, L * NT + t - 1)
                            for a in range(2):
                                for h in range(C_HEADS):
                                    last = nc.tensor.transpose(B(4 + a)[0:QK_C, h * P:(h + 1) * P],
                                                               qk_asm[:, s, a, h, :], ident[:, :])
                                last.then_inc(asm_tr, 1)
                    pe.wait_ge(asm_act, (L + 1) * NT)
                    pe.wait_ge(asm_dve, (L + 1) * NT)
                    pe.wait_ge(o_done["B"], (L + 1) * NU["B"])
                    attend("C", (w_done["C"],))

                    def turn_outputs(t):
                        if t == 0:
                            pe.wait_ge(gab_n, (L + 1) * 2 * NT)
                        pe.wait_ge(gc_n, L * NT + t + 1)
                        if t == 1:
                            pe.wait_ge(o_done["C"], (L + 1) * NU["C"])
                        for j in range(2):
                            q = 2 * t + j
                            if q >= 4:
                                pe.wait_ge(oT_lo, L * 2 * NT + q - 3)
                            cols = [QA, QA + P, QB, QB + P, QB + 2 * P, QB + 3 * P, OC, OC + P]
                            turn_rows(oT_tr, lambda k: p[:, t, cols[k]:cols[k] + P], q, 4 * j)

                    turn_outputs(0)
                    turn_outputs(1)
                    for m in range(2 * NT):
                        half, t = m // NT, m % NT
                        if 1 <= m < NT // 2:
                            turn_outputs(2 * m)
                            turn_outputs(2 * m + 1)
                        pe.wait_ge(oT_lo, L * 2 * NT + 2 * (t + 1))
                        if m >= 4:
                            pe.wait_ge(wadd_done, L * 2 * NT + m - 3)
                        for k in range(NK):
                            u = U_IN + 4 * half + k // 2
                            if t == 0 and k % 2 == 0:
                                pe.wait_ge(split_done, L * U_ALL + u + 1)
                            s = slot_of[u]
                            wcol = slice((k % 2) * HALF, (k % 2 + 1) * HALF)
                            last = three(B(m % 4), hT(k, slice(t * P, (t + 1) * P)),
                                         (W(s)[:, wcol], W(s, True)[:, wcol]), k == 0, k == NK - 1)
                        last.then_inc(wo_done, 1)
                        if half == 1 and t >= 1:
                            norm_turn(2 * L + 1, t - 1)

                    def up(G0, first, c_parity, U0, ufirst):
                        for g in range(4):
                            f, half = g % 2, g // 2
                            if half == 0:
                                pe.wait_ge(split_done, U0 + (ufirst + f + 1))
                            if first:
                                pe.wait_ge(mlo_done, G0 + (first + g - 3))
                            else:
                                pe.wait_ge(wadd_done, L * 2 * NT + (2 * NT - 3 + g))
                                if g == 2:
                                    norm_turn(2 * L + 1, NT - 1)
                                pe.wait_ge(hT_lo_done, (2 * L + 1) * 2 * NT + NT * (half + 1))
                            s = 4 * c_parity + f
                            for k in range(NK):
                                wc = slice(k * P, (k + 1) * P)
                                last = three(B(g), (W(s)[:, wc], W(s, True)[:, wc]),
                                             hT(k, slice(half * HALF, (half + 1) * HALF)), k == 0, k == NK - 1)
                            last.then_inc(mu_done, 1)

                    def down(M0, first, c_parity, G0, gfirst, U0, ufirst):
                        pe.wait_ge(mlo_done, G0 + (gfirst + 4))
                        pe.wait_ge(split_done, U0 + (ufirst + 2))
                        for m in range(16):
                            t, half = m // 2, m % 2
                            if first or m >= 4:
                                pe.wait_ge(madd_done, M0 + (first + m + 13))
                            for f in range(2):
                                s = 4 * c_parity + 2 + f
                                a = 2 * c_parity + f
                                tok = slice(t * P, (t + 1) * P)
                                cols = slice(half * HALF, (half + 1) * HALF)
                                last = three(B(4 + m % 4), (aT_hi[:, a, tok], aT_lo[:, a, tok]),
                                             (W(s)[:, cols], W(s, True)[:, cols]), f == 0, f == 1)
                            last.then_inc(md_done, 1)

                    G, M, U = L * 4 * NC, L * 16 * NC, L * U_ALL
                    up(G, 0, 0, U, U_M)
                    up(G, 4, 1, U, U_M + 4)
                    down(M, 0, 0, G, 0, U, U_M + 2)
                    with pe_engine.Fori(0, NC // 2 - 1) as i_reg:
                        i = Count(0, [(i_reg, 1)])
                        Gi, Mi, Ui = G + 8 * i, M + 32 * i, U + 8 * i
                        for k in range(2):
                            up(Gi, 8 + 4 * k, k, Ui, U_M + 6 + 4 * k)
                            down(Mi, 16 * (k + 1), 1 - k, Gi, 4 * (k + 1), Ui, U_M + 8 + 4 * k)
                    down(M, 16 * (NC - 1), 1, G, 4 * (NC - 1), U, U_ALL - 2)

                pe.wait_ge(consts_in, 4 * 16)
                pe.wait_ge(masks_ready, 3)
                with pe_engine.Fori(0, depth) as L:
                    layer(L, Count(0, [(L, 1)]))


_INS = ["x", "attn_norm", "w_in", "mla_q_norm", "mla_kv_norm", "w_mla_uq", "w_mla_ukv", "sink_logits",
        "group_norm", "w_out", "mlp_norm", "w_mlp_in", "w_mlp_out", "final_norm"]


def shape_constants():
    import numpy as np

    at = np.arange(P)
    causal = np.where(at[None, :] < at[:, None], 0.0, BIG).astype(np.float32)
    chunk = np.where(at[None, :] // HD <= at[:, None] // HD, 0.0, BIG).astype(np.float32)

    def rope(dim):
        inv = (np.float32(1.0) / np.float32(10000.0) ** (np.arange(0, dim, 2, dtype=np.float32) / np.float32(dim)))
        ang = np.arange(S, dtype=np.float32)[:, None] * inv.astype(np.float32)[None, :]
        cos, sin = np.cos(ang).astype(np.float32), np.sin(ang).astype(np.float32)
        tab = np.stack([np.concatenate([cos, cos], 1), np.concatenate([-sin, sin], 1)], 1)
        return np.ascontiguousarray(tab.reshape(NT, P, 2, dim).transpose(1, 0, 2, 3))

    return {"ident": np.eye(P, dtype=np.float32), "causal": causal,
            "chunk": chunk, "rope_b": rope(HD), "rope_c": rope(ROPE_C)}


def kernel(**inputs):
    import numpy as np
    import concourse.bacc as bacc
    from concourse.bass_utils import run_bass_kernel_spmd

    nc = bacc.Bacc("TRN2", target_bir_lowering=False, num_devices=1)
    arrays, args = {}, []
    given = {name: np.ascontiguousarray(inputs[name]) for name in _INS}
    for name, a in {**given, **shape_constants()}.items():
        arrays[f"in_{name}"] = a
        args.append(nc.dram_tensor(f"in_{name}", a.shape, mybir.dt.from_np(a.dtype), kind="ExternalInput").ap())
    args.append(nc.dram_tensor("out", (1, S, D), F32, kind="ExternalOutput").ap())
    hybrid_trunk(nc, *args)
    r = run_bass_kernel_spmd(nc, [arrays], core_ids=[0])
    return r.results[0]["out"]
```
